# Optimizing a Trainium2 kernel written in Bass

```python
import jax
import jax.numpy as jnp
from jax import lax
import numpy as np

D_MODEL = 1024
BATCH = 1
SEQ = 512
DEPTH = 1

ATTN_HEADS = 8
ATTN_HEAD_DIM = 64
ATTN_WIDTH = ATTN_HEADS * ATTN_HEAD_DIM
DILATED_PATTERNS = ((128, 1), (512, 4), (2048, 16))
ATTN_BLOCK = 128
DN_HEADS = 4
DN_HEAD_DIM = 128
DN_WIDTH = DN_HEADS * DN_HEAD_DIM
DN_CHUNK = 64
CONV_WIDTH = 4
MIX_WIDTH = ATTN_WIDTH + DN_WIDTH
IN_SECTIONS = (ATTN_WIDTH, ATTN_WIDTH, ATTN_WIDTH, DN_WIDTH, DN_WIDTH, DN_WIDTH, DN_HEADS, DN_HEADS, DN_WIDTH)
IN_COLS = sum(IN_SECTIONS)
D_FF = 2816
NORM_EPS = 1e-6
L2_EPS = 1e-6
INIT_NOISE = 0.02

kernel_name = "hybrid_dilated_attn_gated_deltanet_macaron"

def rms_norm(x, gain):
    xf = x.astype(jnp.float32)
    y = xf * lax.rsqrt(jnp.mean(xf * xf, axis=-1, keepdims=True) + NORM_EPS)
    return (y * gain.astype(jnp.float32)).astype(x.dtype)

def swiglu(h, w_gate, w_up, w_down):
    return (jax.nn.silu(h @ w_gate) * (h @ w_up)) @ w_down

def alibi_slopes(n_heads):
    return jnp.asarray(np.array([2.0 ** (-8.0 * (i + 1) / n_heads) for i in range(n_heads)], dtype=np.float32))

def dilated_window_attention(q, k, v, slopes, window, dilation):
    B, S, H, Dh = q.shape
    L = S // dilation
    W = window // dilation
    nb = -(-L // ATTN_BLOCK)
    Lp = nb * ATTN_BLOCK

    def residues(t):
        return t.reshape(B, L, dilation, H, Dh).transpose(0, 2, 3, 1, 4).reshape(B * dilation, H, L, Dh)

    qr = jnp.pad(residues(q), ((0, 0), (0, 0), (0, Lp - L), (0, 0))).reshape(B * dilation, H, nb, ATTN_BLOCK, Dh)

    def band(t):
        t = jnp.pad(residues(t), ((0, 0), (0, 0), (ATTN_BLOCK, Lp - L), (0, 0)))
        t = t.reshape(B * dilation, H, nb + 1, ATTN_BLOCK, Dh)
        return jnp.concatenate([t[:, :, :-1], t[:, :, 1:]], axis=3)

    kb, vb = band(k), band(v)
    s = jnp.einsum('zhnqd,zhnkd->zhnqk', qr, kb) * (Dh ** -0.5)
    qi = jnp.arange(ATTN_BLOCK)[:, None]
    kj = jnp.arange(2 * ATTN_BLOCK)[None, :]
    steps = qi + ATTN_BLOCK - kj
    key_idx = jnp.arange(nb)[:, None, None] * ATTN_BLOCK + kj - ATTN_BLOCK
    valid = (steps >= 0) & (steps <= W) & (key_idx >= 0)
    bias = -slopes[:, None, None, None] * (steps * dilation).astype(jnp.float32)
    s = jnp.where(valid, s + bias, -jnp.inf)
    m = jnp.max(s, axis=-1)
    p = jnp.exp(s - m[..., None])
    l = jnp.sum(p, axis=-1)
    o = jnp.einsum('zhnqk,zhnkd->zhnqd', p, vb) / l[..., None]

    def back(t):
        extra = t.shape[4:]
        t = t.reshape(B, dilation, H, Lp, *extra)[:, :, :, :L]
        perm = (0, 3, 1, 2) + tuple(range(4, 4 + len(extra)))
        return t.transpose(perm).reshape(B, S, H, *extra)

    return back(o), back(m), back(l)

def dilated_attention(q, k, v):
    slopes = alibi_slopes(q.shape[2])
    outs, maxes, denoms = [], [], []
    for window, dilation in DILATED_PATTERNS:
        o, m, l = dilated_window_attention(q, k, v, slopes, window, dilation)
        outs.append(o)
        maxes.append(m)
        denoms.append(l)
    m_all = jnp.stack(maxes)
    wts = jnp.stack(denoms) * jnp.exp(m_all - jnp.max(m_all, axis=0, keepdims=True))
    return jnp.einsum('pbsh,pbshd->bshd', wts, jnp.stack(outs)) / jnp.sum(wts, axis=0)[..., None]

def gated_delta_rule(q, k, v, beta, g):
    B, S, H, Dk = q.shape
    Dv = v.shape[-1]
    C = DN_CHUNK
    N = S // C

    def chunks(t):
        return jnp.moveaxis(t.reshape(B, N, C, H, *t.shape[3:]), 3, 1)

    q = chunks(q) * (Dk ** -0.5)
    k, v, beta = chunks(k), chunks(v), chunks(beta)
    g = jnp.cumsum(chunks(g), axis=-1)
    causal = jnp.tril(jnp.ones((C, C), dtype=bool))
    strict = jnp.tril(jnp.ones((C, C), dtype=bool), k=-1)
    decay = jnp.exp(jnp.where(causal, g[..., :, None] - g[..., None, :], -jnp.inf))
    k_beta = k * beta[..., None]
    a_mat = jnp.where(strict, jnp.einsum('bhnck,bhnjk->bhncj', k_beta, k) * decay, 0.0)
    eye = jnp.eye(C, dtype=q.dtype)
    rhs = jnp.concatenate([v * beta[..., None], k_beta * jnp.exp(g)[..., None]], axis=-1)
    sol = lax.linalg.triangular_solve(eye + a_mat, rhs, left_side=True, lower=True)
    u, w = sol[..., :Dv], sol[..., Dv:]
    attn_intra = jnp.where(causal, jnp.einsum('bhnck,bhnjk->bhncj', q, k) * decay, 0.0)

    def step(state, xs):
        q_n, k_n, u_n, w_n, g_n, a_n = xs
        v_new = u_n - jnp.einsum('bhck,bhkv->bhcv', w_n, state)
        o_n = (jnp.einsum('bhck,bhkv->bhcv', q_n * jnp.exp(g_n)[..., None], state)
               + jnp.einsum('bhcj,bhjv->bhcv', a_n, v_new))
        g_last = g_n[..., -1]
        k_dec = k_n * jnp.exp(g_last[..., None] - g_n)[..., None]
        state = state * jnp.exp(g_last)[..., None, None] + jnp.einsum('bhck,bhcv->bhkv', k_dec, v_new)
        return state, o_n

    xs = tuple(jnp.moveaxis(t, 2, 0) for t in (q, k, u, w, g, attn_intra))
    state0 = jnp.zeros((B, H, Dk, Dv), q.dtype)
    _, o = lax.scan(step, state0, xs)
    return o.transpose(1, 0, 3, 2, 4).reshape(B, S, H, Dv)

def hybrid_mixer(h, w_in, conv_w, a_log, dt_bias, dn_norm, w_out):
    B, S, _ = h.shape
    f32 = jnp.float32
    split_points = np.cumsum(IN_SECTIONS)[:-1].tolist()
    aq, ak, av, dq, dk, dv, beta_raw, decay_raw, gate = jnp.split(h @ w_in, split_points, axis=-1)

    def attn_heads(t):
        return t.reshape(B, S, ATTN_HEADS, ATTN_HEAD_DIM).astype(f32)

    attn = dilated_attention(attn_heads(aq), attn_heads(ak), attn_heads(av))
    attn = attn.reshape(B, S, ATTN_WIDTH).astype(h.dtype)

    qkv = jnp.concatenate([dq, dk, dv], axis=-1)
    qkv_pad = jnp.pad(qkv, ((0, 0), (CONV_WIDTH - 1, 0), (0, 0)))
    conv = qkv_pad[:, 0:S] * conv_w[0]
    for j in range(1, CONV_WIDTH):
        conv = conv + qkv_pad[:, j:j + S] * conv_w[j]
    dq, dk, dv = jnp.split(jax.nn.silu(conv).astype(f32), 3, axis=-1)

    def dn_heads(t):
        return t.reshape(B, S, DN_HEADS, DN_HEAD_DIM)

    def l2n(t):
        return t * lax.rsqrt(jnp.sum(t * t, axis=-1, keepdims=True) + L2_EPS)

    beta = jax.nn.sigmoid(beta_raw.astype(f32))
    g = -jnp.exp(a_log.astype(f32)) * jax.nn.softplus(decay_raw.astype(f32) + dt_bias.astype(f32))
    o = gated_delta_rule(l2n(dn_heads(dq)), l2n(dn_heads(dk)), dn_heads(dv), beta, g)
    o = (o * lax.rsqrt(jnp.mean(o * o, axis=-1, keepdims=True) + NORM_EPS) * dn_norm.astype(f32)
         * jax.nn.silu(dn_heads(gate.astype(f32))))
    dn = o.reshape(B, S, DN_WIDTH).astype(h.dtype)

    return jnp.concatenate([attn, dn], axis=-1) @ w_out

def setup_inputs(seed: int = 0) -> dict:
    key = jax.random.key(seed)
    ks = jax.random.split(key, 17)
    f32 = jnp.float32
    L = DEPTH

    def normal(k, shape, scale):
        return jax.random.normal(k, shape, f32) * scale

    def gain(k, shape):
        return 1.0 + INIT_NOISE * jax.random.normal(k, shape, f32)

    dt = jnp.exp(jax.random.uniform(ks[9], (L, DN_HEADS), f32, float(np.log(1e-3)), float(np.log(1e-1))))
    return {
        "x": normal(ks[0], (BATCH, SEQ, D_MODEL), 1.0),
        "norm_ffn1": gain(ks[1], (L, D_MODEL)),
        "ffn1_gate": normal(ks[2], (L, D_MODEL, D_FF), D_MODEL ** -0.5),
        "ffn1_up": normal(ks[3], (L, D_MODEL, D_FF), D_MODEL ** -0.5),
        "ffn1_down": normal(ks[4], (L, D_FF, D_MODEL), D_FF ** -0.5),
        "norm_mix": gain(ks[5], (L, D_MODEL)),
        "w_in": normal(ks[6], (L, D_MODEL, IN_COLS), D_MODEL ** -0.5),
        "conv_w": normal(ks[7], (L, CONV_WIDTH, 3 * DN_WIDTH), CONV_WIDTH ** -0.5),
        "a_log": jnp.log(jax.random.uniform(ks[8], (L, DN_HEADS), f32, 1.0, 16.0)),
        "dt_bias": dt + jnp.log(-jnp.expm1(-dt)),
        "dn_norm": gain(ks[10], (L, DN_HEAD_DIM)),
        "w_out": normal(ks[11], (L, MIX_WIDTH, D_MODEL), MIX_WIDTH ** -0.5),
        "norm_ffn2": gain(ks[12], (L, D_MODEL)),
        "ffn2_gate": normal(ks[13], (L, D_MODEL, D_FF), D_MODEL ** -0.5),
        "ffn2_up": normal(ks[14], (L, D_MODEL, D_FF), D_MODEL ** -0.5),
        "ffn2_down": normal(ks[15], (L, D_FF, D_MODEL), D_FF ** -0.5),
        "norm_final": gain(ks[16], (D_MODEL,)),
    }

def reference(x, norm_ffn1, ffn1_gate, ffn1_up, ffn1_down, norm_mix, w_in, conv_w, a_log, dt_bias,
              dn_norm, w_out, norm_ffn2, ffn2_gate, ffn2_up, ffn2_down, norm_final):
    for i in range(DEPTH):
        x = x + 0.5 * swiglu(rms_norm(x, norm_ffn1[i]), ffn1_gate[i], ffn1_up[i], ffn1_down[i])
        x = x + hybrid_mixer(rms_norm(x, norm_mix[i]), w_in[i], conv_w[i], a_log[i], dt_bias[i],
                             dn_norm[i], w_out[i])
        x = x + 0.5 * swiglu(rms_norm(x, norm_ffn2[i]), ffn2_gate[i], ffn2_up[i], ffn2_down[i])
    return rms_norm(x, norm_final)


_drawn_inputs = setup_inputs


def setup_inputs(seed=0):
    import zlib

    import numpy as np

    out = dict(_drawn_inputs(seed))
    spreads = {}
    factors = {'norm_ffn1': 5.484,
     'norm_mix': 3.799,
     'dn_norm': 6.454,
     'norm_ffn2': 7.997,
     'norm_final': 2.861}
    for name, (base, spread) in spreads.items():
        noise = np.random.default_rng([zlib.crc32(name.encode()), seed]).standard_normal(out[name].shape)
        drawn = base * np.exp(spread * noise) if base else spread * noise
        out[name] = jnp.asarray(drawn.astype(out[name].dtype))
    for name, factor in factors.items():
        out[name] = (out[name] * factor).astype(out[name].dtype)
    return out
```

```python
from contextlib import ExitStack

import numpy as np

import concourse.bass as bass
from concourse import mybir

F32 = mybir.dt.float32
F32R = mybir.dt.float32r
ALU = mybir.AluOpType
ACT = mybir.ActivationFunctionType
AX_X = mybir.AxisListType.X

P = 128
D, S, F = 1024, 512, 2816
KD, NT, KF = D // P, S // P, F // P
AH, ADH = 8, 64
NH, DH, CH = 4, 128, 64
AW, DW = AH * ADH, NH * DH
COL = dict(aq=0, ak=AW, av=2 * AW, dq=3 * AW, dk=3 * AW + DW, dv=3 * AW + 2 * DW,
           beta=3 * AW + 3 * DW, gate=3 * AW + 3 * DW + 2 * NH)
PATTERNS = ((128, 1), (512, 4), (2048, 16))
CONV = 4
EPS = 1e-6
LEVELS = 6
MASKED = -1e30

RAWS, SPLITS, AHEAD = 2, 4, 2
FFN_SLOTS = 3 * KF
UNITS = [("dk", h) for h in range(NH)] + [("dq", h) for h in range(NH)] + [("dv", h) for h in range(NH)]


def mixer_slots():
    out = [("T", s, h) for s, h in UNITS]
    for s in ("av", "gate"):
        out += [("N", s, j) for j in range(KD // 2)]
    for p in range(AH // 2):
        out += [("T", "aq", p), ("T", "ak", p)]
    for half in range(2):
        out += [("O", half, j) for j in (2, 3, 0, 1)]
    return out


MSLOTS = mixer_slots()
BASE = [0, FFN_SLOTS + len(MSLOTS)]
MBASE = FFN_SLOTS
NSLOTS = 2 * FFN_SLOTS + len(MSLOTS)


def tile_steps(i):
    out = [("t1", c, i) for c in "kqv"] + [("t2", c, i) for c in "kq"] + [("gb", i), ("gram", i), ("l1t", i)]
    for lev in range(1, LEVELS):
        out += [("W", i, lev), ("PQ", i, lev)]
    return out + [("uw", i)]


def chunk_steps(i):
    out = []
    for n in (2 * i, 2 * i + 1):
        out += [("chA", n), ("chS", n), ("chO", n)]
    return out + [("out", i), ("outT", i)]


def spread(a, b):
    out, j = [], 0
    for i, x in enumerate(a):
        out.append(x)
        while j < len(b) and (j + 1) * len(a) <= (i + 1) * len(b):
            out.append(b[j])
            j += 1
    return out + b[j:]


def attention_steps(p):
    ms = [(h, q) for h in (2 * p, 2 * p + 1) for q in range(NT)]
    out = []
    for n in range(len(ms) + 2):
        if n < len(ms):
            out.append(("aS", *ms[n]))
        if n >= 2:
            out.append(("aV", *ms[n - 2]))
        if 1 <= n <= len(ms):
            out.append(("aT", *ms[n - 1]))
    return out + [("aO", p)]


def mixer_order():
    def fill(j):
        return [("fill", j, q) for q in range(4)]

    out = []
    for j, _ in enumerate(UNITS):
        out += fill(j) + [("conv", j)]
        if j >= 1:
            out.append(("silu", j - 1))
    out.append(("silu", len(UNITS) - 1))
    first = len(UNITS)
    dn = tile_steps(0)
    for i in range(1, NT):
        dn += spread(tile_steps(i), chunk_steps(i - 1))
    dn += chunk_steps(NT - 1)
    flow = []
    for j in range(first, first + KD):
        flow += fill(j)
        if j == first + KD // 2 - 1:
            flow.append(("avs",))
        if j == first + KD - 1:
            flow.append(("gates",))
    for p in range(AH // 2):
        j = first + KD + 2 * p
        own = fill(j) + [("qk", p, 0)] + fill(j + 1) + [("qk", p, 1)]
        flow += spread(own, attention_steps(p - 1)) if p else own
    n_fill = flow.index(("gates",))
    cut = dn.index(("chO", 0))
    merged = spread(flow, dn)
    if merged.index(("chO", 0)) < merged.index(("gates",)):
        merged = spread(flow[:n_fill + 1], dn[:cut]) + spread(flow[n_fill + 1:], dn[cut:])
    out += merged
    out += [("ysplit", k) for k in range(4, 8)]
    j = first + KD + AH
    tail = fill(j) + fill(j + 1)
    out += spread(attention_steps(AH // 2 - 1), tail)
    out += [("ysplit", k) for k in range(0, 4)]
    for k in range(j + 2, j + 8):
        out += fill(k)
    return out


ORDER = mixer_order()


def plan_banks():
    use, count, up = {}, [0] * 8, []

    def take(key, bank):
        count[bank] += 1
        use[key] = (bank, count[bank])

    def norm(n):
        for t in range(NT):
            for half in range(2):
                take(("xT", n, t, half), 2 * t + half)

    def ffn(f):
        up.append(list(count[:4]))
        for b in range(4):
            count[b] += KF // 2
        for t in range(NT):
            for half in range(2):
                take(("y", f, t, half), 2 * t + half)

    norm(0)
    ffn(0)
    norm(1)
    turn = [0]

    def rotate(key):
        take(key, 4 + turn[0] % 3)
        turn[0] += 1

    for key in (("cw",), ("bd",), ("gc",)):
        rotate(key)
    for step in ORDER:
        kind = step[0]
        if kind == "fill" and step[2] == 0:
            what, sec, j = MSLOTS[step[1]]
            if what == "T":
                take(("T", step[1]), step[1] % 2)
            elif what == "N" and j == 0:
                for t in range(NT):
                    take(("N", sec, t), t)
            elif what == "O" and j == 2:
                for t in range(NT):
                    take(("o", sec, t), 4 * sec + t)
        elif kind in ("t1", "t2", "gb", "l1t", "W", "chA", "chS", "outT", "aS", "aT"):
            rotate(step)
        elif kind == "gram":
            rotate(("kk", step[1]))
            rotate(("kq", step[1]))
        elif kind == "PQ":
            if step[2] < LEVELS - 1:
                rotate(("P", *step[1:]))
            rotate(("Q", *step[1:]))
        elif kind == "uw":
            rotate(("u", step[1]))
            rotate(("w", step[1]))
        elif kind == "chO" and step[1] % 2 == 0:
            take(("PO", step[1] // 2), 3)
        elif kind == "aV" and step[1] % 2 == 0 and step[2] == 0:
            take(("O", step[1] // 2), 7)
    norm(2)
    ffn(1)
    return use, up


USE, UP_BASE = plan_banks()


def shape_tables():
    r = np.arange(P)
    row, col = r[:, None], r[None, :]
    chunk = row // CH == col // CH
    parts = [np.eye(P), chunk & (row <= col), chunk,
             np.where(chunk & (col <= row), 0.0, MASKED), np.where(chunk & (row <= col), 0.0, MASKED)]
    for lev in range(LEVELS):
        b = 1 << lev
        parts.append((row // (2 * b) == col // (2 * b)) & (row // b % 2 == 1) & (col // b % 2 == 0))
    table = np.concatenate([np.asarray(x, np.float32) for x in parts], axis=1)
    dist = row + (S - P) - np.arange(S)[None, :]
    times = sum(((dist >= 0) & (dist % d == 0) & (dist // d <= w // d)).astype(np.int64) for w, d in PATTERNS)
    base = np.where(times > 0, np.log(np.maximum(times, 1)), MASKED)
    slopes = [2.0 ** (-8.0 * (i + 1) / AH) for i in range(AH)]
    bias = np.stack([(base - s * dist) * ADH ** 0.5 for s in slopes])
    return table, bias.astype(np.float32)


def decoder_layer(nc, A, out):
    ctx = ExitStack()
    with ctx:
        start = (nc.sbuf_base + 31) // 32 * 32
        at = [start]

        def sb(name, shape, dt=F32):
            n = 4 * int(np.prod(shape[1:]))
            h = nc.alloc_sbuf_tensor_at(name, shape, dt, offset=at[0])
            at[0] += (n + 31) // 32 * 32
            return h

        w_raw = sb("w_raw", [P, RAWS, 1024])
        w_hi = sb("w_hi", [P, SPLITS, 1024], F32R)
        w_lo = sb("w_lo", [P, SPLITS, 1024], F32R)
        xT_hi = sb("xT_hi", [P, KD, S], F32R)
        xT_lo = sb("xT_lo", [P, KD, S], F32R)
        table = sb("table", [P, 5 + LEVELS, P])
        gain = sb("gain", [P, D])
        ssq = sb("ssq", [P, 16])
        rstd = sb("rstd", [P, 16])
        minus_half = sb("minus_half", [P, 1])
        conv_w = sb("conv_w", [P, CONV * len(UNITS)])
        conv_rows = sb("conv_rows", [CONV * len(UNITS), P])
        wbd = sb("wbd", [P, KD, 2 * NH])
        wbd_hi = sb("wbd_hi", [P, KD, 2 * NH], F32R)
        wbd_lo = sb("wbd_lo", [P, KD, 2 * NH], F32R)
        dtb = sb("dtb", [P, NH])
        alog = sb("alog", [P, NH])
        dnn = sb("dnn", [P, DH])
        gt = {n: sb("g_" + n, [P, NT, NH]) for n in
              ("z", "zn", "mz", "e", "ln", "g", "eb", "beta", "eg", "ekd", "beg", "ngc", "gd")}
        gcum = sb("gcum", [P, 2, NT, NH])
        expa = sb("expa", [P, NH])
        ss_qk = sb("ss_qk", [P, 2, NH])
        rn_qk = sb("rn_qk", [P, 2, NH])
        egl = sb("egl", [P, 2, NH, 2])
        ss_o = sb("ss_o", [P, NH])
        ms_o = sb("ms_o", [P, NH])
        rs_o = sb("rs_o", [P, NH])
        nmax = sb("nmax", [P, AH * NT])
        den = sb("den", [P, AH * NT])
        rden = sb("rden", [P, AH * NT])
        arena = at[0]
        x = sb("x", [P, NT, D])
        after_x = at[0]
        hT = sb("hT", [P, KF, S])
        h_hi = sb("h_hi", [P, 2, S], F32R)
        h_lo = sb("h_lo", [P, 2, S], F32R)
        sg = sb("sg", [P, 2, S])
        xs = sb("xs", [P, 2, D])
        assert at[0] <= nc.sbuf_usable_end
        at[0] = arena
        av = sb("av", [P, NT, AW])
        gs = sb("gs", [P, NT, DW])
        assert at[0] <= after_x
        sil = sb("sil", [P, len(UNITS), S])
        kT = sb("kT", [P, NH, P])
        qT = sb("qT", [P, NH, P])
        vb = sb("vb", [P, NH, DH])
        kbeg = sb("kbeg", [P, NH, DH])
        kdec = sb("kdec", [P, 2, NH, DH])
        qgT = sb("qgT", [P, 2, NH, P])
        egbc = sb("egbc", [P, NH, P])
        dec = sb("dec", [P, NH, P])
        decT = sb("decT", [P, NH, P])
        Am = sb("Am", [P, NH, P])
        Lm = sb("Lm", [P, 2, NH, P])
        Di = sb("Di", [P, NH, P])
        DiT = sb("DiT", [P, NH, P])
        Wm = sb("Wm", [P, NH, P])
        attnT = sb("attnT", [P, 2, NH, P])
        u = sb("u", [P, NH, DH])
        wT = sb("wT", [P, NH, P])
        vnew = sb("vnew", [P, NH, DH])
        St = sb("St", [P, 2, NH, DH])
        y = sb("y", [P, NH, DH])
        qk = sb("qk", [P, 2, 2, S])
        pr = sb("pr", [P, 2, S])
        ab = sb("ab", [P, 2, S])
        yT = sb("yT", [P, KD, S])
        assert at[0] <= nc.sbuf_usable_end, at[0] - nc.sbuf_usable_end
        pT = gain
        kn, qn = DiT, Di
        x_kept = nc.dram_tensor("x_kept", [S, D], F32, kind="Internal").ap().rearrange("(t p) d -> p t d", p=P)

        ident, upto, same = table[:, 0, :], table[:, 1, :], table[:, 2, :]
        neg, negT = table[:, 3:4, :], table[:, 4:5, :]
        bank = [ctx.enter_context(nc.psum_tensor(f"bank{b}", [P, 512], F32)) for b in range(8)]

        def per_head(ap):
            return ap.rearrange("p (h c) -> p h c", h=NH)

        def over(ap, n=P):
            return ap.unsqueeze(2).broadcast_to([P, NH, n])

        def sem(name):
            return ctx.enter_context(nc.semaphore(name))

        filled = [sem(f"filled{b}") for b in range(8)]
        drained = [sem(f"drained{b}") for b in range(8)]
        raw_landed = [sem(f"raw_landed{r}") for r in range(RAWS)]
        hi_done = sem("hi_done")
        split_done = sem("split_done")
        slots_begun = sem("slots_begun")
        x_landed = [sem(f"x_landed{t}") for t in range(NT)]
        tables_landed = sem("tables_landed")
        small_landed = sem("small_landed")
        bias_landed = [sem(f"bias_landed{b}") for b in range(2)]
        gain_landed = sem("gain_landed")
        x_spilled = sem("x_spilled")
        x_back = sem("x_back")
        stored = [sem(f"stored{b}") for b in range(2)]
        half_set = sem("half_set")
        sq_done = sem("sq_done")
        rstd_done = sem("rstd_done")
        xs_done = sem("xs_done")
        xT_rounded = sem("xT_rounded")
        h_rounded = sem("h_rounded")
        h_split = sem("h_split")
        small_split = sem("small_split")
        gate_math = sem("gate_math")
        silu_done = sem("silu_done")
        norm_squared = sem("norm_squared")
        norm_summed = sem("norm_summed")
        norm_rooted = sem("norm_rooted")
        k_scaled = sem("k_scaled")
        q_decayed = sem("q_decayed")
        bcast_exp = sem("bcast_exp")
        dec_done = sem("dec_done")
        L_done = sem("L_done")
        Di_done = sem("Di_done")
        state_zero = sem("state_zero")
        o_squared = sem("o_squared")
        o_summed = sem("o_summed")
        o_rooted = sem("o_rooted")
        y_done = sem("y_done")
        gate_silu = sem("gate_silu")
        gate_gained = sem("gate_gained")
        exp_done = sem("exp_done")
        probs_done = sem("probs_done")
        y_rounded = sem("y_rounded")
        y_split = sem("y_split")
        dve_own = sem("dve_own")
        act_own = sem("act_own")
        pool_own = sem("pool_own")

        def open_bank(eng, key):
            b, n = USE[key]
            if n > 1:
                eng.wait_ge(drained[b], n - 1)
            return bank[b]

        def wait_filled(eng, key):
            b, n = USE[key]
            eng.wait_ge(filled[b], n)
            return bank[b]

        def wait_drained(eng, key):
            b, n = USE[key]
            eng.wait_ge(drained[b], n)

        def full(key):
            return filled[USE[key][0]]

        def drain(key):
            return drained[USE[key][0]]

        def wait_added(eng, r, t):
            for half in range(2):
                wait_drained(eng, ("o", half, t) if r == 1 else ("y", r // 2, t, half))

        w_in = A["w_in"][0].rearrange("(k p) n -> p k n", p=P)
        w_out = A["w_out"][0].rearrange("(k p) n -> p k n", p=P)
        gates_in = [A[n][0].rearrange("(k p) n -> p k n", p=P) for n in ("ffn1_gate", "ffn2_gate")]
        ups_in = [A[n][0].rearrange("(k p) n -> p k n", p=P) for n in ("ffn1_up", "ffn2_up")]
        downs_in = [A[n][0] for n in ("ffn1_down", "ffn2_down")]
        x_in = A["x"][0].rearrange("(t p) d -> p t d", p=P)
        out_v = out[0].rearrange("(t p) d -> p t d", p=P)
        gains = [A["norm_ffn1"], A["norm_mix"], A["norm_ffn2"], A["norm_final"]]

        block = ctx.enter_context(nc.Block())

        @block.sync
        def _(sp):
            def load(w, ring, src, split):
                sp.wait_ge(split_done, w + 1)
                dst = w_raw[:, ring, :]
                if split > 1:
                    dst = dst.rearrange("p (k n) -> p k n", k=split)
                sp.dma_start(dst, src).then_inc(raw_landed[ring], 16)

            for t in range(NT):
                sp.dma_start(x[:, t, :], x_in[:, t, :]).then_inc(x_landed[t], 16)
                if t == 0:
                    sp.dma_start(table[:], A["table"].rearrange("p (m n) -> p m n", n=P)).then_inc(tables_landed, 16)

            def ffn_stream(f):
                with sp.Fori(0, KF // 2) as i:
                    for c in range(2):
                        for g, src in enumerate((gates_in[f], ups_in[f])):
                            load(BASE[f] + 4 * i + 2 * c + g, g,
                                 src[:, :, bass.ds(i * 256 + c * 128, P)], KD)
                base = BASE[f] + 2 * KF
                with sp.Fori(0, KF // 2) as i:
                    for c in range(2):
                        load(base + 2 * i + c, c, downs_in[f][bass.ds(i * 256 + c * 128, P), :], 1)

            ffn_stream(0)
            for j, (what, sec, n) in enumerate(MSLOTS):
                if j == 2:
                    sp.wait_ge(xs_done, 2 * NT)
                    sp.dma_start(x_kept, x[:]).then_inc(x_spilled, 16)
                if j == len(MSLOTS) - 4:
                    wait_filled(sp, ("O", AH // 2 - 1))
                    sp.wait_ge(y_done, NT)
                    sp.wait_ge(x_spilled, 16)
                    sp.dma_start(x[:], x_kept).then_inc(x_back, 16)
                w = MBASE + j
                if what == "T":
                    load(w, w % RAWS, w_in[:, :, COL[sec] + n * P:COL[sec] + (n + 1) * P], KD)
                elif what == "N":
                    load(w, w % RAWS, w_in[:, 2 * n:2 * n + 2, COL[sec]:COL[sec] + 512], 2)
                else:
                    load(w, w % RAWS, w_out[:, 2 * n:2 * n + 2, sec * 512:(sec + 1) * 512], 2)
            ffn_stream(1)
            for t in range(NT):
                sp.wait_ge(xs_done, 3 * NT + t + 1)
                sp.dma_start(out_v[:, t, :], xs[:, t % 2, :]).then_inc(stored[t % 2], 16)
            for b in range(2):
                sp.wait_ge(stored[b], 16 * NT // 2)

        @block.scalar
        def _(act):
            own = [0]

            def link(ins):
                own[0] += 1
                ins.then_inc(act_own, 1)
                act.wait_ge(act_own, own[0])

            def round_slot(w, ring, waits=True):
                act.wait_ge(raw_landed[ring % RAWS], 16 * (w // RAWS) + 16)
                if waits:
                    act.wait_ge(slots_begun, w - 2)
                act.activation(w_hi[:, ring, :], w_raw[:, ring % RAWS, :], ACT.Copy).then_inc(hi_done, 1)

            def round_looped(base, i, per, off):
                w0 = base + off
                act.wait_ge(raw_landed[w0 % RAWS], 16 * (per // RAWS) * i + 16 * (w0 // RAWS) + 16)
                act.wait_ge(slots_begun, per * i + (w0 - 2))
                act.activation(w_hi[:, w0 % SPLITS, :], w_raw[:, w0 % RAWS, :], ACT.Copy).then_inc(hi_done, 1)

            def square(n, t):
                if n == 0:
                    act.wait_ge(x_landed[t], 16)
                else:
                    wait_added(act, n - 1, t)
                if t >= 2:
                    if n < 3:
                        wait_filled(act, ("xT", n, t - 2, 1))
                    else:
                        act.wait_ge(stored[t % 2], 16)
                act.activation(xs[:, t % 2, :], x[:, t, :], ACT.Square,
                               accum_out=ssq[:, 4 * n + t:4 * n + t + 1]).then_inc(sq_done, 1)

            def norm(n):
                for t in range(NT):
                    square(n, t)
                    if t >= 1:
                        round_x(n, t - 1)
                round_x(n, NT - 1)

            def round_x(n, t):
                for half in range(2):
                    ps = wait_filled(act, ("xT", n, t, half))
                    act.activation(xT_hi[:, 4 * half:4 * half + 4, t * P:(t + 1) * P],
                                   per_head(ps[:]), ACT.Copy).then_inc(xT_rounded, 1)

            def ffn(f):
                b, n = BASE[f], UP_BASE[f]
                with act.Fori(0, KF // 2) as i:
                    for c in range(2):
                        round_looped(b, i, 4, 2 * c + 2)
                        round_looped(b, i, 4, 2 * c + 3)
                        act.wait_ge(filled[2 * c], i + n[2 * c] + 1)
                        act.wait_ge(drained[2 * c + 1], i + n[2 * c + 1])
                        act.activation(sg[:, c, :], bank[2 * c][:], ACT.Silu).then_inc(drained[2 * c], 1)
                act.wait_ge(drained[1], n[1] + 1)
                act.activation(h_hi[:, 0, :], hT[:, 0, :], ACT.Copy).then_inc(h_rounded, 1)
                act.wait_ge(drained[3], n[3] + KF // 2)

                b = BASE[f] + 2 * KF

                for kt in range(2):
                    round_slot(b + kt + AHEAD, (b + kt + AHEAD) % SPLITS)
                    act.wait_ge(slots_begun, b + kt + 1)
                    act.activation(h_hi[:, (kt + 1) % 2, :], hT[:, kt + 1, :], ACT.Copy).then_inc(h_rounded, 1)
                with act.Fori(0, 4) as i:
                    for c in range(4):
                        round_looped(b, i, 4, 2 + c + AHEAD)
                        act.wait_ge(slots_begun, 4 * i + (b + 2 + c + 1))
                        act.activation(h_hi[:, (3 + c) % 2, :],
                                       hT[:].rearrange("p k n -> p (k n)")[:, bass.ds(i * (4 * S) + (3 + c) * S, S)],
                                       ACT.Copy).then_inc(h_rounded, 1)
                for kt in range(18, KF):
                    if b + kt + AHEAD < NSLOTS:
                        round_slot(b + kt + AHEAD, (b + kt + AHEAD) % SPLITS)
                    if kt + 1 < KF:
                        act.wait_ge(slots_begun, b + kt + 1)
                        act.activation(h_hi[:, (kt + 1) % 2, :], hT[:, kt + 1, :], ACT.Copy).then_inc(h_rounded, 1)

            def mixer():
                wait_filled(act, ("xT", 1, NT - 1, 1))
                for h in range(2):
                    act.dma_start(ab[:, h, :], A["bias"][h]).then_inc(bias_landed[h], 16)
                act.wait_ge(small_landed, 16 * 5)
                act.activation(wbd_hi[:], wbd[:], ACT.Copy).then_inc(small_split, 1)
                act.wait_ge(gate_math, 1)
                ps = bank[USE[("bd",)][0]]
                act.activation(gt["eb"][:], ps[:, 0:NT * 2 * NH].rearrange("p (t n) -> p t n", t=NT)[:, :, 0:NH],
                               ACT.Exp, scale=-1.0).then_inc(drain(("bd",)), 1)
                act.activation(expa[:], alog[:], ACT.Exp)
                act.wait_ge(gate_math, 2)
                link(act.activation(gt["e"][:], gt["e"][:], ACT.Exp))
                act.activation(gt["ln"][:], gt["e"][:], ACT.Ln, bias=1.0).then_inc(gate_math, 1)
                act.wait_ge(gate_math, 5)
                act.activation(gt["eg"][:], gcum[:, 0, :, :], ACT.Exp)
                act.activation(gt["ekd"][:], gt["gd"][:], ACT.Exp).then_inc(gate_math, 1)

                for step in ORDER:
                    kind = step[0]
                    if kind == "fill":
                        w = MBASE + step[1] + AHEAD
                        if step[2] == 0:
                            round_slot(w, w % SPLITS)
                    elif kind == "silu":
                        wait_drained(act, ("T", step[1]))
                        act.activation(sil[:, step[1], :], sil[:, step[1], :], ACT.Silu).then_inc(silu_done, 1)
                    elif kind == "avs":
                        act.wait_ge(x_spilled, 16)
                        for t in range(NT):
                            ps = wait_filled(act, ("N", "av", t))
                            act.activation(av[:, t, :], ps[:], ACT.Copy).then_inc(drain(("N", "av", t)), 1)
                    elif kind == "gates":
                        act.wait_ge(x_spilled, 16)
                        for t in range(NT):
                            ps = wait_filled(act, ("N", "gate", t))
                            act.activation(gs[:, t, :], ps[:], ACT.Silu).then_inc(drain(("N", "gate", t)), 1)
                    elif kind == "qk":
                        key = ("T", len(UNITS) + KD + 2 * step[1] + step[2])
                        ps = wait_filled(act, key)
                        act.activation(qk[:, step[1] % 2, step[2], :], ps[:], ACT.Copy).then_inc(drain(key), 1)
                    elif kind == "t1" and step[1] != "v":
                        i, to = step[2], dec if step[1] == "k" else decT
                        if i >= 1:
                            wait_drained(act, ("kq", i - 1))
                        ps = wait_filled(act, step)
                        act.activation(to[:], per_head(ps[:]), ACT.Square).then_inc(norm_squared, 1)
                    elif kind == "t2":
                        i = step[2]
                        if step[1] == "q" and i >= 1:
                            act.wait_ge(q_decayed, i)
                        ps = wait_filled(act, step)
                        act.activation((kT if step[1] == "k" else qT)[:], per_head(ps[:]), ACT.Copy)\
                           .then_inc(drain(step), 1)
                    elif kind == "gb":
                        i = step[1]
                        ps = wait_filled(act, step)
                        if i >= 1:
                            act.wait_ge(q_decayed, i)
                        if i >= 2:
                            wait_drained(act, ("chS", 2 * i - 3))
                        act.activation(egl[:, i % 2, :, :],
                                       ps[:].rearrange("p (h c j) -> p h c j", h=NH, c=2)[:, :, :, CH - 1], ACT.Exp)
                        act.activation(egbc[:], per_head(ps[:]), ACT.Exp).then_inc(bcast_exp, 1)
                        wait_drained(act, step)
                        for h in range(NH):
                            act.activation(dec[:, h, :], dec[:, h, :], ACT.Exp, bias=gcum[:, 0, i, h:h + 1])
                        for h in range(NH):
                            last = act.activation(decT[:, h, :], decT[:, h, :], ACT.Exp, bias=gt["ngc"][:, i, h:h + 1])
                        last.then_inc(dec_done, 1)
                    elif kind == "W":
                        ps = wait_filled(act, step)
                        act.activation(Wm[:], per_head(ps[:]), ACT.Copy).then_inc(drain(step), 1)
                    elif kind == "uw":
                        i = step[1]
                        if i >= 1:
                            wait_drained(act, ("chA", 2 * i - 1))
                        ps = wait_filled(act, ("u", i))
                        act.activation(u[:], per_head(ps[:]), ACT.Copy).then_inc(drain(("u", i)), 1)
                        ps = wait_filled(act, ("w", i))
                        act.activation(wT[:], per_head(ps[:]), ACT.Copy).then_inc(drain(("w", i)), 1)
                    elif kind == "out":
                        i = step[1]
                        if i >= 1:
                            wait_filled(act, ("outT", i - 1))
                        ps = wait_filled(act, ("PO", i))
                        act.activation(y[:], per_head(ps[:]), ACT.Square).then_inc(o_squared, 1)
                    elif kind == "outT":
                        i = step[1]
                        ps = wait_filled(act, step)
                        act.activation(yT[:, AW // P:, i * P:(i + 1) * P], per_head(ps[:]), ACT.Copy)\
                           .then_inc(drain(step), 1)
                    elif kind == "aS":
                        h, q = step[1:]
                        m, n = NT * h + q, (q + 1) * P
                        wait_drained(act, step)
                        act.activation(pr[:, m % 2, 0:n], pr[:, m % 2, 0:n], ACT.Exp, scale=-1.0,
                                       bias=nmax[:, m:m + 1], accum_out=den[:, m:m + 1]).then_inc(exp_done, 1)
                        if q == NT - 1 and h + 2 < AH:
                            act.dma_start(ab[:, h % 2, :], A["bias"][h + 2]).then_inc(bias_landed[h % 2], 16)
                    elif kind == "aT":
                        ps = wait_filled(act, step)
                        n = (step[2] + 1) * P
                        act.activation(pT[:, 0:n], ps[:, 0:n], ACT.Copy).then_inc(drain(step), 1)
                    elif kind == "ysplit":
                        k = step[1]
                        if k == 4:
                            wait_filled(act, ("T", len(UNITS) + KD + AH - 1))
                        wait_drained(act, ("outT", NT - 1) if k >= 4 else ("O", k))
                        act.activation(xT_hi[:, k, :], yT[:, k, :], ACT.Copy).then_inc(y_rounded, 1)

            act.dma_start(wbd[:], w_in[:, :, COL["beta"]:COL["beta"] + 2 * NH]).then_inc(small_landed, 16)
            act.dma_start(conv_rows[:], A["conv_w"][0].rearrange("j (u p) -> (j u) p", p=P)).then_inc(small_landed, 16)
            act.dma_start(dtb[:], A["dt_bias"][0:1, :].broadcast_to([P, NH])).then_inc(small_landed, 16)
            act.dma_start(alog[:], A["a_log"][0:1, :].broadcast_to([P, NH])).then_inc(small_landed, 16)
            act.dma_start(dnn[:], A["dn_norm"][0:1, :].broadcast_to([P, DH])).then_inc(small_landed, 16)
            for w in range(AHEAD):
                round_slot(w, w, waits=False)
            norm(0)
            ffn(0)
            norm(1)
            mixer()
            norm(2)
            ffn(1)
            for t in range(NT):
                square(3, t)

        @block.vector
        def _(dve):
            own = [0]

            def link(ins):
                own[0] += 1
                ins.then_inc(dve_own, 1)
                dve.wait_ge(dve_own, own[0])

            def rest_of_slot(w, ring):
                dve.wait_ge(hi_done, w + 1)
                dve.tensor_tensor(w_lo[:, ring, :], w_raw[:, ring % RAWS, :], w_hi[:, ring, :].bitcast(F32),
                                  ALU.subtract).then_inc(split_done, 1)

            def scale_x(n, t):
                if t == 0:
                    dve.wait_ge(gain_landed, 16 * (n + 1))
                dve.wait_ge(rstd_done, NT * n + t + 1)
                dve.scalar_tensor_tensor(out=xs[:, t % 2, :], in0=x[:, t, :], scalar=rstd[:, 4 * n + t:4 * n + t + 1],
                                         in1=gain[:], op0=ALU.mult, op1=ALU.mult).then_inc(xs_done, 1)

            def rest_of_x(n, t):
                for half in range(2):
                    key = ("xT", n, t, half)
                    dve.wait_ge(xT_rounded, 8 * n + 2 * t + half + 1)
                    dve.tensor_tensor(xT_lo[:, 4 * half:4 * half + 4, t * P:(t + 1) * P],
                                      per_head(bank[USE[key][0]][:]),
                                      xT_hi[:, 4 * half:4 * half + 4, t * P:(t + 1) * P].bitcast(F32),
                                      ALU.subtract).then_inc(drain(key), 1)

            def norm(n, branch=None):
                for t in range(NT):
                    if branch is not None:
                        for half in range(2):
                            add_half(branch, t, half)
                    scale_x(n, t)
                    if t >= 1:
                        rest_of_x(n, t - 1)
                rest_of_x(n, NT - 1)

            def add_half(f, t, half):
                key = ("y", f, t, half)
                ps = wait_filled(dve, key)
                part = x[:, t, half * 512:(half + 1) * 512]
                dve.scalar_tensor_tensor(out=part, in0=ps[:], scalar=0.5, in1=part,
                                         op0=ALU.mult, op1=ALU.add).then_inc(drain(key), 1)

            def ffn(f):
                b, n = BASE[f], UP_BASE[f]
                dve.wait_ge(split_done, b + AHEAD + RAWS)
                with dve.Fori(0, KF // 2) as i:
                    for c in range(2):
                        rest_of_slot(4 * i + (b + 2 * c + 2), (b + 2 * c + 2) % SPLITS)
                        rest_of_slot(4 * i + (b + 2 * c + 3), (b + 2 * c + 3) % SPLITS)
                        dve.wait_ge(drained[2 * c], i + n[2 * c] + 1)
                        dve.wait_ge(filled[2 * c + 1], i + n[2 * c + 1] + 1)
                        dve.tensor_tensor(hT[:].rearrange("p k n -> p (k n)")[:, bass.ds(i * (2 * S) + c * S, S)],
                                          sg[:, c, :], bank[2 * c + 1][:], ALU.mult).then_inc(drained[2 * c + 1], 1)
                h0 = f * KF
                dve.wait_ge(drained[3], n[3] + KF // 2)
                dve.wait_ge(h_rounded, h0 + 1)
                dve.tensor_tensor(h_lo[:, 0, :], hT[:, 0, :], h_hi[:, 0, :].bitcast(F32), ALU.subtract)\
                   .then_inc(h_split, 1)
                b = BASE[f] + 2 * KF

                def rest_of_h(value, k, src):
                    dve.wait_ge(h_rounded, value)
                    dve.tensor_tensor(h_lo[:, k % 2, :], src, h_hi[:, k % 2, :].bitcast(F32), ALU.subtract)\
                       .then_inc(h_split, 1)

                for kt in range(2):
                    rest_of_slot(b + kt + AHEAD, (b + kt + AHEAD) % SPLITS)
                    rest_of_h(h0 + kt + 2, kt + 1, hT[:, kt + 1, :])
                with dve.Fori(0, 4) as i:
                    for c in range(4):
                        rest_of_slot(4 * i + (b + 2 + c + AHEAD), (b + 2 + c + AHEAD) % SPLITS)
                        rest_of_h(4 * i + (h0 + 2 + c + 2), 3 + c,
                                  hT[:].rearrange("p k n -> p (k n)")[:, bass.ds(i * (4 * S) + (3 + c) * S, S)])
                for kt in range(18, KF):
                    if b + kt + AHEAD < NSLOTS:
                        rest_of_slot(b + kt + AHEAD, (b + kt + AHEAD) % SPLITS)
                    if kt + 1 < KF:
                        rest_of_h(h0 + kt + 2, kt + 1, hT[:, kt + 1, :])

            def mixer():
                dve.wait_ge(small_split, 1)
                dve.tensor_tensor(wbd_lo[:], wbd[:], wbd_hi[:].bitcast(F32), ALU.subtract).then_inc(small_split, 1)
                ps = wait_filled(dve, ("cw",))
                dve.tensor_copy(conv_w[:], ps[:, 0:CONV * len(UNITS)]).then_inc(drain(("cw",)), 1)
                ps = wait_filled(dve, ("bd",))
                raw = ps[:, 0:NT * 2 * NH].rearrange("p (t n) -> p t n", t=NT)
                wide = [P, NT, NH]
                ins = dve.tensor_tensor(gt["z"][:], raw[:, :, NH:2 * NH], dtb[:].unsqueeze(1).broadcast_to(wide), ALU.add)
                ins.then_inc(gate_math, 1)
                dve.wait_ge(gate_math, 1)
                link(dve.tensor_scalar(gt["zn"][:], gt["z"][:], -1.0, None, ALU.mult))
                dve.tensor_tensor(gt["e"][:], gt["z"][:], gt["zn"][:], ALU.min).then_inc(gate_math, 1)
                link(dve.tensor_scalar(gt["mz"][:], gt["z"][:], 0.0, None, ALU.max))
                dve.wait_ge(gate_math, 3)
                link(dve.tensor_tensor(gt["zn"][:], gt["mz"][:], gt["ln"][:], ALU.add))
                dve.scalar_tensor_tensor(out=gt["g"][:], in0=gt["zn"][:], scalar=-1.0,
                                         in1=expa[:].unsqueeze(1).broadcast_to(wide), op0=ALU.mult, op1=ALU.mult)\
                   .then_inc(gate_math, 1)
                wait_drained(dve, ("bd",))
                link(dve.tensor_scalar(gt["eb"][:], gt["eb"][:], 1.0, None, ALU.add))
                link(dve.reciprocal(gt["beta"][:], gt["eb"][:]))
                ps = wait_filled(dve, ("gc",))
                link(dve.tensor_copy(gcum[:].rearrange("p a t n -> p (a t n)"), ps[:, 0:2 * NT * NH]))
                dve.tensor_scalar(gt["ngc"][:], gcum[:, 0, :, :], -1.0, None, ALU.mult).then_inc(drain(("gc",)), 1)
                dve.tensor_tensor(gt["gd"][:], gcum[:, 1, :, :], gcum[:, 0, :, :], ALU.subtract).then_inc(gate_math, 1)
                dve.wait_ge(gate_math, 6)
                dve.tensor_tensor(gt["beg"][:], gt["beta"][:], gt["eg"][:], ALU.mult).then_inc(gate_math, 1)

                sums = [0]
                for step in ORDER:
                    kind = step[0]
                    if kind == "conv":
                        j = step[1]
                        sec, h = UNITS[j]
                        unit = {"dq": 0, "dk": NH, "dv": 2 * NH}[sec] + h
                        ps = wait_filled(dve, ("T", j))
                        w = [conv_w[:, c * len(UNITS) + unit:c * len(UNITS) + unit + 1] for c in range(CONV)]
                        if j == 0:
                            wait_drained(dve, ("cw",))
                        link(dve.tensor_scalar(sil[:, j, :], ps[:], w[CONV - 1], None, ALU.mult))
                        for back in range(1, CONV):
                            part = sil[:, j, back:S]
                            ins = dve.scalar_tensor_tensor(out=part, in0=ps[:, 0:S - back], scalar=w[CONV - 1 - back],
                                                           in1=part, op0=ALU.mult, op1=ALU.add)
                            if back < CONV - 1:
                                link(ins)
                        ins.then_inc(drain(("T", j)), 1)
                    elif kind == "gates":
                        for t in range(NT):
                            wait_drained(dve, ("N", "gate", t))
                            dve.tensor_tensor(per_head(gs[:, t, :]), per_head(gs[:, t, :]),
                                              dnn[:].unsqueeze(1).broadcast_to([P, NH, DH]), ALU.mult)\
                               .then_inc(gate_gained, 1)
                    elif kind == "t1" and step[1] != "v":
                        c, i = "kq".index(step[1]), step[2]
                        sq = (dec, decT)[c]
                        dve.wait_ge(norm_squared, 2 * i + c + 1)
                        if i >= 1:
                            dve.wait_ge(norm_rooted, 2 * (i - 1) + c + 1)
                        link(dve.tensor_reduce(ss_qk[:, c, :], sq[:], AX_X, ALU.add))
                        dve.tensor_scalar(ss_qk[:, c, :], ss_qk[:, c, :], EPS, None, ALU.add).then_inc(norm_summed, 1)
                        dve.wait_ge(norm_rooted, 2 * i + c + 1)
                        ps = bank[USE[step][0]]
                        if i >= 1 and c == 0:
                            dve.wait_ge(k_scaled, 2 * i)
                        dve.scalar_tensor_tensor(out=(kn, qn)[c][:], in0=per_head(ps[:]),
                                                 scalar=(1.0, DH ** -0.5)[c], in1=over(rn_qk[:, c, :]),
                                                 op0=ALU.mult, op1=ALU.mult).then_inc(drain(step), 1)
                    elif kind == "t1":
                        i = step[2]
                        ps = wait_filled(dve, step)
                        dve.tensor_tensor(vb[:], per_head(ps[:]), over(gt["beta"][:, i, :]), ALU.mult)\
                           .then_inc(drain(step), 1)
                    elif kind == "gb":
                        i = step[1]
                        dve.wait_ge(bcast_exp, i + 1)
                        ps = bank[USE[step][0]]
                        dve.tensor_tensor(dec[:], neg.broadcast_to([P, NH, P]), per_head(ps[:]), ALU.subtract)
                        dve.tensor_tensor(decT[:], negT.broadcast_to([P, NH, P]), per_head(ps[:]), ALU.add)\
                           .then_inc(drain(step), 1)
                    elif kind == "gram":
                        i = step[1]
                        ps = wait_filled(dve, ("kk", i))
                        dve.wait_ge(dec_done, i + 1)
                        if i >= 1:
                            dve.wait_ge(L_done, LEVELS * i)
                        for h in range(NH):
                            ins = dve.scalar_tensor_tensor(out=Am[:, h, :], in0=ps[:, h * P:(h + 1) * P],
                                                           scalar=gt["beta"][:, i, h:h + 1], in1=dec[:, h, :],
                                                           op0=ALU.mult, op1=ALU.mult)
                        ins.then_inc(drain(("kk", i)), 1)
                        ps = wait_filled(dve, ("kq", i))
                        dve.tensor_tensor(attnT[:, i % 2, :, :], per_head(ps[:]), decT[:], ALU.mult)\
                           .then_inc(drain(("kq", i)), 1)
                    elif kind == "l1t":
                        i = step[1]
                        ps = wait_filled(dve, step)
                        dve.tensor_tensor(DiT[:], ident.unsqueeze(1).broadcast_to([P, NH, P]), per_head(ps[:]),
                                          ALU.subtract).then_inc(drain(step), 1)
                        dve.tensor_tensor(Di[:], ident.unsqueeze(1).broadcast_to([P, NH, P]), Lm[:, 0, :, :],
                                          ALU.subtract).then_inc(Di_done, 1)
                    elif kind == "PQ":
                        i, lev = step[1:]
                        ps_q = wait_filled(dve, ("Q", i, lev))
                        if lev < LEVELS - 1:
                            ps = bank[USE[("P", i, lev)][0]]
                            dve.wait_ge(Di_done, i + 1)
                            if lev > 1:
                                wait_drained(dve, ("P", i, lev - 1))
                            dve.tensor_tensor(Di[:], Di[:], per_head(ps[:]), ALU.subtract)\
                               .then_inc(drain(("P", i, lev)), 1)
                        wait_drained(dve, ("Q", i, lev - 1) if lev > 1 else ("l1t", i))
                        dve.tensor_tensor(DiT[:], DiT[:], per_head(ps_q[:]), ALU.subtract)\
                           .then_inc(drain(("Q", i, lev)), 1)
                    elif kind == "chA":
                        n = step[1]
                        r = slice(CH * (n % 2), CH * (n % 2) + CH)
                        wait_drained(dve, ("u", n // 2))
                        ps = wait_filled(dve, step)
                        dve.tensor_tensor(vnew[r, :, :], u[r, :, :], ps[r, :].rearrange("p (h c) -> p h c", h=NH),
                                          ALU.subtract).then_inc(drain(step), 1)
                    elif kind == "chS":
                        n = step[1]
                        ps = wait_filled(dve, step)
                        if n == 0:
                            dve.wait_ge(state_zero, 1)
                        else:
                            wait_drained(dve, ("chS", n - 1))
                        for h in range(NH):
                            ins = dve.scalar_tensor_tensor(
                                out=St[:, (n + 1) % 2, h, :], in0=St[:, n % 2, h, :],
                                scalar=egl[:, n // 2 % 2, h, n % 2:n % 2 + 1], in1=ps[:, h * P:(h + 1) * P],
                                op0=ALU.mult, op1=ALU.add)
                        ins.then_inc(drain(step), 1)
                    elif kind == "out":
                        i = step[1]
                        dve.wait_ge(o_squared, i + 1)
                        link(dve.tensor_reduce(ss_o[:], y[:], AX_X, ALU.add))
                        if i >= 1:
                            dve.wait_ge(o_rooted, i)
                        dve.tensor_scalar(ms_o[:], ss_o[:], 1.0 / DH, EPS, ALU.mult, ALU.add).then_inc(o_summed, 1)
                        dve.wait_ge(o_rooted, i + 1)
                        ps = bank[USE[("PO", i)][0]]
                        ins = dve.tensor_tensor(y[:], per_head(ps[:]), over(rs_o[:]), ALU.mult)
                        ins.then_inc(drain(("PO", i)), 1)
                        wait_drained(dve, ("PO", i))
                        dve.wait_ge(gate_gained, i + 1)
                        dve.tensor_tensor(y[:], y[:], per_head(gs[:, i, :]), ALU.mult).then_inc(y_done, 1)
                    elif kind == "aS":
                        h, q = step[1:]
                        m, n = NT * h + q, (q + 1) * P
                        ps = wait_filled(dve, step)
                        if q == 0:
                            dve.wait_ge(bias_landed[h % 2], 16 * (h // 2 + 1))
                        dve.tensor_tensor_reduce(out=pr[:, m % 2, 0:n], in0=ps[:, 0:n], in1=ab[:, h % 2, S - n:S],
                                                 scale=-(ADH ** -0.5), scalar=3e38, op0=ALU.add, op1=ALU.min,
                                                 accum_out=nmax[:, m:m + 1]).then_inc(drain(step), 1)
                    elif kind == "aT":
                        h, q = step[1:]
                        m, n = NT * h + q, (q + 1) * P
                        dve.wait_ge(exp_done, m + 1)
                        link(dve.reciprocal(rden[:, m:m + 1], den[:, m:m + 1]))
                        dve.tensor_scalar(pr[:, m % 2, 0:n], pr[:, m % 2, 0:n], rden[:, m:m + 1], None, ALU.mult)\
                           .then_inc(probs_done, 1)
                    elif kind == "aO":
                        ps = wait_filled(dve, ("O", step[1]))
                        dve.tensor_copy(yT[:, step[1], :], ps[:]).then_inc(drain(("O", step[1])), 1)
                    elif kind == "ysplit":
                        k = step[1]
                        sums[0] += 1
                        dve.wait_ge(y_rounded, sums[0])
                        dve.tensor_tensor(xT_lo[:, k, :], yT[:, k, :], xT_hi[:, k, :].bitcast(F32), ALU.subtract)\
                           .then_inc(y_split, 1)
                dve.wait_ge(x_back, 16)
                for t in range(NT):
                    ps = wait_filled(dve, ("o", 0, t))
                    dve.tensor_tensor(x[:, t, 0:512], x[:, t, 0:512], ps[:], ALU.add).then_inc(drain(("o", 0, t)), 1)

            def norm_after_mixer():
                for t in range(NT):
                    ps = wait_filled(dve, ("o", 1, t))
                    dve.tensor_tensor(x[:, t, 512:], x[:, t, 512:], ps[:], ALU.add).then_inc(drain(("o", 1, t)), 1)
                for t in range(NT):
                    scale_x(2, t)
                    if t >= 1:
                        rest_of_x(2, t - 1)
                rest_of_x(2, NT - 1)

            dve.memset(ms_o[:], 0.0).then_inc(split_done, RAWS)
            for w in range(AHEAD):
                rest_of_slot(w, w)
            norm(0)
            ffn(0)
            norm(1, branch=0)
            mixer()
            norm_after_mixer()
            ffn(1)
            for t in range(NT):
                for half in range(2):
                    add_half(1, t, half)
                scale_x(3, t)

        @block.gpsimd
        def _(pool):
            own = [0]

            def link(ins):
                own[0] += 1
                ins.then_inc(pool_own, 1)
                pool.wait_ge(pool_own, own[0])

            def root(out_ap, in_ap, n):
                return pool.tensor_tensor(out_ap, in_ap, minus_half[:, 0:1].broadcast_to([P, n]), ALU.pow)

            def load_gain(n):
                if n:
                    pool.wait_ge(xs_done, NT * n)
                if n == 2:
                    wait_filled(pool, ("O", AH // 2 - 1))
                src = gains[n][0:1, :] if n < 3 else gains[n].rearrange("(a d) -> a d", a=1)
                pool.dma_start(gain[:], src.broadcast_to([P, D])).then_inc(gain_landed, 16)

            def norm(n):
                load_gain(n)
                for t in range(NT):
                    c = slice(4 * n + t, 4 * n + t + 1)
                    pool.wait_ge(sq_done, NT * n + t + 1)
                    link(pool.tensor_scalar(ssq[:, c], ssq[:, c], 1.0 / D, EPS, ALU.mult, ALU.add))
                    root(rstd[:, c], ssq[:, c], 1).then_inc(rstd_done, 1)

            def rest_of_slot(w):
                ring = w % SPLITS
                pool.wait_ge(hi_done, w + 1)
                pool.tensor_tensor(w_lo[:, ring, :], w_raw[:, ring % RAWS, :], w_hi[:, ring, :].bitcast(F32),
                                   ALU.subtract).then_inc(split_done, 1)

            def mask(i, lev):
                if lev == 0:
                    wait_drained(pool, ("kk", i))
                if lev == 2:
                    pool.wait_ge(Di_done, i + 1)
                    wait_filled(pool, ("l1t", i))
                if lev >= 3:
                    wait_filled(pool, ("W", i, lev - 2))
                pool.tensor_tensor(Lm[:, lev % 2, :, :], Am[:],
                                   table[:, 5 + lev:6 + lev, :].broadcast_to([P, NH, P]), ALU.mult).then_inc(L_done, 1)

            def mixer():
                pool.wait_ge(split_done, MBASE + AHEAD + RAWS)
                wait_filled(pool, ("cw",))
                pool.wait_ge(xs_done, 2 * NT)
                wait_filled(pool, ("xT", 1, NT - 1, 1))
                pool.memset(St[:, 0, :, :], 0.0).then_inc(state_zero, 1)
                for step in ORDER:
                    kind = step[0]
                    if kind == "fill" and step[2] == 0:
                        rest_of_slot(MBASE + step[1] + AHEAD)
                    elif kind == "t1" and step[1] != "v":
                        c, i = "kq".index(step[1]), step[2]
                        pool.wait_ge(norm_summed, 2 * i + c + 1)
                        root(rn_qk[:, c, :], ss_qk[:, c, :], NH).then_inc(norm_rooted, 1)
                    elif kind == "t2" and step[1] == "k":
                        i = step[2]
                        wait_drained(pool, ("t1", "k", i))
                        if i == 0:
                            pool.wait_ge(gate_math, 7)
                        pool.tensor_tensor(kbeg[:], kn[:], over(gt["beg"][:, i, :]), ALU.mult).then_inc(k_scaled, 1)
                        pool.tensor_tensor(kdec[:, i % 2, :, :], kn[:], over(gt["ekd"][:, i, :]), ALU.mult)\
                            .then_inc(k_scaled, 1)
                    elif kind == "gb":
                        i = step[1]
                        wait_drained(pool, ("t2", "q", i))
                        pool.wait_ge(bcast_exp, i + 1)
                        pool.tensor_tensor(qgT[:, i % 2, :, :], qT[:], egbc[:], ALU.mult).then_inc(q_decayed, 1)
                    elif kind == "gram":
                        mask(step[1], 0)
                        mask(step[1], 1)
                    elif kind == "W" and step[2] < LEVELS - 1:
                        mask(step[1], step[2] + 1)
                    elif kind == "out":
                        i = step[1]
                        pool.wait_ge(o_summed, i + 1)
                        root(rs_o[:], ms_o[:], NH).then_inc(o_rooted, 1)

            pool.memset(minus_half[:], -0.5).then_inc(half_set, 1)
            pool.wait_ge(half_set, 1)
            norm(0)
            norm(1)
            mixer()
            norm(2)
            norm(3)

        @block.tensor
        def _(pe):
            def three(ps, s_hi, s_lo, m_hi, m_lo, start, stop):
                first = pe.matmul(ps, s_hi, m_hi, start=start, stop=False)
                pe.matmul(ps, s_hi, m_lo, start=False, stop=False)
                return first, pe.matmul(ps, s_lo, m_hi, start=False, stop=stop)

            def transpose_x(n, t):
                pe.wait_ge(xs_done, NT * n + t + 1)
                for half in range(2):
                    key = ("xT", n, t, half)
                    ps = open_bank(pe, key)
                    for j in range(4):
                        k = 4 * half + j
                        ins = pe.transpose(ps[:, j * P:(j + 1) * P], xs[:, t % 2, k * P:(k + 1) * P], ident)
                    ins.then_inc(full(key), 1)

            def x_split(n):
                for t in range(NT):
                    for half in range(2):
                        wait_drained(pe, ("xT", n, t, half))

            def ffn(f):
                b, n = BASE[f], UP_BASE[f]
                x_split(2 * f)
                with pe.Fori(0, KF // 2) as i:
                    for c in range(2):
                        for g in range(2):
                            w, k0 = b + 2 * c + g, 2 * c + g
                            pe.wait_ge(split_done, 4 * i + (w + 1 + RAWS))
                            pe.wait_ge(drained[k0], i + n[k0])
                            for k in range(KD):
                                s = slice(k * P, (k + 1) * P)
                                first, last = three(bank[k0][:], w_hi[:, w % SPLITS, s], w_lo[:, w % SPLITS, s],
                                                    xT_hi[:, k, :], xT_lo[:, k, :], k == 0, k == KD - 1)
                                if k == 0:
                                    first.then_inc(slots_begun, 1)
                            last.then_inc(filled[k0], 1)
                b, h0 = BASE[f] + 2 * KF, f * KF

                def step(kt, t, start=False, stop=False, begins=False):
                    r = (b + kt) % SPLITS
                    hh, hl = (v[:, kt % 2, t * P:(t + 1) * P] for v in (h_hi, h_lo))
                    for part, (s, m) in enumerate(((hh, w_hi), (hh, w_lo), (hl, w_hi))):
                        for half in range(2):
                            ins = pe.matmul(bank[2 * t + half][:], s, m[:, r, half * 512:(half + 1) * 512],
                                            start=start and part == 0, stop=stop and part == 2)
                            if begins and part == 0 and half == 0:
                                ins.then_inc(slots_begun, 1)
                            if stop and part == 2:
                                ins.then_inc(filled[2 * t + half], 1)

                def whole(kt, value_slot, value_h, start=False):
                    pe.wait_ge(split_done, value_slot)
                    pe.wait_ge(h_split, value_h)
                    for t in (2, 3, 0, 1):
                        if start:
                            for half in range(2):
                                open_bank(pe, ("y", f, t, half))
                        step(kt, t, start=start, begins=t == 2)

                for kt in range(2):
                    whole(kt, b + kt + 1 + RAWS, h0 + kt + 1, start=kt == 0)
                with pe.Fori(0, 4) as i:
                    for c in range(4):
                        whole(2 + c, 4 * i + (b + 2 + c + 1 + RAWS), 4 * i + (h0 + 2 + c + 1))
                for kt in (18, 19):
                    whole(kt, b + kt + 1 + RAWS, h0 + kt + 1)
                pe.wait_ge(split_done, b + KF - 1 + RAWS)
                pe.wait_ge(h_split, h0 + KF - 1)
                for t in range(NT):
                    step(20, t, begins=t == 0)
                    if t == 0:
                        pe.wait_ge(split_done, b + KF + RAWS)
                        pe.wait_ge(h_split, h0 + KF)
                    step(21, t, stop=True, begins=t == NT - 1)
                    if f == 0 and t >= 2:
                        transpose_x(1, t - 2)

            def fill(j, quarter):
                w = MBASE + j
                r = w % SPLITS
                what, sec, n = MSLOTS[j]
                if quarter == 0:
                    pe.wait_ge(split_done, w + 1 + RAWS)
                if what == "T":
                    key = ("T", j)
                    ps = open_bank(pe, key) if quarter == 0 else bank[USE[key][0]]
                    for k in (2 * quarter, 2 * quarter + 1):
                        s = slice(k * P, (k + 1) * P)
                        first, last = three(ps[:], w_hi[:, r, s], w_lo[:, r, s], xT_hi[:, k, :], xT_lo[:, k, :],
                                            k == 0, k == KD - 1)
                        if k == 0:
                            first.then_inc(slots_begun, 1)
                    if quarter == 3:
                        last.then_inc(full(key), 1)
                    return
                kk = quarter // 2
                k = 2 * n + kk
                k_first, k_last = (0, KD - 1) if what == "N" else (4, 3)
                if what == "O" and quarter == 0:
                    pe.wait_ge(y_split, {2: 2, 3: 4, 0: 6, 1: 8}[n])
                for t in (0, 1) if quarter % 2 == 0 else (2, 3):
                    key = ("N", sec, t) if what == "N" else ("o", sec, t)
                    ps = open_bank(pe, key) if k == k_first else bank[USE[key][0]]
                    s = slice(t * P, (t + 1) * P)
                    m = slice(kk * 512, (kk + 1) * 512)
                    first, last = three(ps[:], xT_hi[:, k, s], xT_lo[:, k, s], w_hi[:, r, m], w_lo[:, r, m],
                                        k == k_first, k == k_last)
                    if quarter == 0 and t == 0:
                        first.then_inc(slots_begun, 1)
                    if k == k_last:
                        last.then_inc(full(key), 1)

            def heads(step, product):
                ps = open_bank(pe, step)
                for h in range(NH):
                    ins = product(ps[:, h * P:(h + 1) * P], h)
                ins.then_inc(full(step), 1)

            def one(ps, s, m):
                return pe.matmul(ps, s, m, start=True, stop=True)

            def mixer():
                ps = open_bank(pe, ("cw",))
                n = CONV * len(UNITS)
                pe.wait_ge(small_landed, 16 * 5)
                pe.transpose(ps[:, 0:n], conv_rows[:], table[0:n, 0, 0:n]).then_inc(full(("cw",)), 1)
                x_split(1)
                ps = open_bank(pe, ("bd",))
                pe.wait_ge(small_split, 2)
                for t in range(NT):
                    for k in range(KD):
                        s = slice(t * P, (t + 1) * P)
                        _, last = three(ps[:, t * 2 * NH:(t + 1) * 2 * NH], xT_hi[:, k, s], xT_lo[:, k, s],
                                        wbd_hi[:, k, :], wbd_lo[:, k, :], k == 0, k == KD - 1)
                last.then_inc(full(("bd",)), 1)
                ps = open_bank(pe, ("gc",))
                pe.wait_ge(gate_math, 4)
                g = gt["g"][:].rearrange("p t n -> p (t n)")
                one(ps[:, 0:NT * NH], upto, g)
                one(ps[:, NT * NH:2 * NT * NH], same, g).then_inc(full(("gc",)), 1)

                for step in ORDER:
                    kind = step[0]
                    if kind == "fill":
                        fill(step[1], step[2])
                    elif kind == "t1":
                        c, i = step[1:]
                        first = UNITS.index(("d" + c, 0))
                        pe.wait_ge(silu_done, first + NH)
                        heads(step, lambda ps, h: pe.transpose(ps, sil[:, first + h, i * P:(i + 1) * P], ident))
                    elif kind == "t2":
                        c, i = step[1:]
                        wait_drained(pe, ("t1", c, i))
                        heads(step, lambda ps, h: pe.transpose(ps, (kn if c == "k" else qn)[:, h, :], ident))
                    elif kind == "gb":
                        i = step[1]
                        heads(step, lambda ps, h: one(ps, gt["g"][:, i, h:h + 1].broadcast_to([P, P]), upto))
                    elif kind == "gram":
                        i = step[1]
                        wait_drained(pe, ("t2", "k", i))
                        wait_drained(pe, ("t2", "q", i))
                        heads(("kk", i), lambda ps, h: one(ps, kT[:, h, :], kT[:, h, :]))
                        heads(("kq", i), lambda ps, h: one(ps, kT[:, h, :], qT[:, h, :]))
                    elif kind == "l1t":
                        i = step[1]
                        pe.wait_ge(L_done, LEVELS * i + 1)
                        heads(step, lambda ps, h: pe.transpose(ps, Lm[:, 0, h, :], ident))
                    elif kind == "W":
                        i, lev = step[1:]
                        pe.wait_ge(L_done, LEVELS * i + lev + 1)
                        wait_drained(pe, ("Q", i, lev - 1) if lev > 1 else ("l1t", i))
                        heads(step, lambda ps, h: one(ps, Lm[:, lev % 2, h, :], DiT[:, h, :]))
                    elif kind == "PQ":
                        i, lev = step[1:]
                        wait_drained(pe, ("W", i, lev))
                        pe.wait_ge(Di_done, i + 1)
                        if lev > 1:
                            wait_drained(pe, ("P", i, lev - 1))
                        if lev < LEVELS - 1:
                            heads(("P", i, lev), lambda ps, h: one(ps, Wm[:, h, :], Di[:, h, :]))
                        heads(("Q", i, lev), lambda ps, h: one(ps, Di[:, h, :], Wm[:, h, :]))
                    elif kind == "uw":
                        i = step[1]
                        wait_drained(pe, ("Q", i, LEVELS - 1))
                        wait_drained(pe, ("t1", "v", i))
                        heads(("u", i), lambda ps, h: one(ps, DiT[:, h, :], vb[:, h, :]))
                        pe.wait_ge(k_scaled, 2 * i + 1)
                        heads(("w", i), lambda ps, h: one(ps, kbeg[:, h, :], DiT[:, h, :]))
                    elif kind == "chA":
                        n = step[1]
                        r = slice(CH * (n % 2), CH * (n % 2) + CH)
                        wait_drained(pe, ("w", n // 2))
                        if n == 0:
                            pe.wait_ge(state_zero, 1)
                        else:
                            wait_drained(pe, ("chS", n - 1))
                        ps = open_bank(pe, step)
                        for h in range(NH):
                            ins = one(ps[r, h * DH:(h + 1) * DH], wT[:, h, r], St[:, n % 2, h, :])
                        ins.then_inc(full(step), 1)
                    elif kind == "chS":
                        n = step[1]
                        r = slice(CH * (n % 2), CH * (n % 2) + CH)
                        wait_drained(pe, ("chA", n))
                        pe.wait_ge(k_scaled, 2 * (n // 2) + 2)
                        heads(step, lambda ps, h: one(ps, kdec[r, n // 2 % 2, h, :], vnew[r, h, :]))
                    elif kind == "chO":
                        n = step[1]
                        i = n // 2
                        r = slice(CH * (n % 2), CH * (n % 2) + CH)
                        pe.wait_ge(q_decayed, i + 1)
                        wait_drained(pe, ("kq", i))
                        key = ("PO", i)
                        ps = open_bank(pe, key) if n % 2 == 0 else bank[USE[key][0]]
                        for h in range(NH):
                            cols = slice(h * DH, (h + 1) * DH)
                            pe.matmul(ps[r, cols], qgT[:, i % 2, h, r], St[:, n % 2, h, :], start=True, stop=False)
                            ins = pe.matmul(ps[r, cols], attnT[r, i % 2, h, r], vnew[r, h, :], start=False, stop=True)
                        if n % 2 == 1:
                            ins.then_inc(full(key), 1)
                    elif kind == "outT":
                        pe.wait_ge(y_done, step[1] + 1)
                        heads(step, lambda ps, h: pe.transpose(ps, y[:, h, :], ident))
                    elif kind == "aS":
                        h, q = step[1:]
                        pair, r = h // 2, slice(ADH * (h % 2), ADH * (h % 2) + ADH)
                        wait_drained(pe, ("T", len(UNITS) + KD + 2 * pair))
                        wait_drained(pe, ("T", len(UNITS) + KD + 2 * pair + 1))
                        ps = open_bank(pe, step)
                        one(ps[:, 0:(q + 1) * P], qk[r, pair % 2, 0, q * P:(q + 1) * P],
                            qk[r, pair % 2, 1, 0:(q + 1) * P]).then_inc(full(step), 1)
                    elif kind == "aT":
                        h, q = step[1:]
                        m = NT * h + q
                        pe.wait_ge(probs_done, m + 1)
                        ps = open_bank(pe, step)
                        for kb in range(q + 1):
                            ins = pe.transpose(ps[:, kb * P:(kb + 1) * P], pr[:, m % 2, kb * P:(kb + 1) * P], ident)
                        ins.then_inc(full(step), 1)
                    elif kind == "aV":
                        h, q = step[1:]
                        pair, r = h // 2, slice(ADH * (h % 2), ADH * (h % 2) + ADH)
                        key = ("O", pair)
                        ps = open_bank(pe, key) if h % 2 == 0 and q == 0 else bank[USE[key][0]]
                        wait_drained(pe, ("aT", h, q))
                        wait_drained(pe, ("N", "av", NT - 1))
                        for kb in range(q + 1):
                            ins = pe.matmul(ps[r, q * P:(q + 1) * P], av[:, kb, h * ADH:(h + 1) * ADH],
                                            pT[:, kb * P:(kb + 1) * P], start=kb == 0, stop=kb == q)
                        if h % 2 == 1 and q == NT - 1:
                            ins.then_inc(full(key), 1)

            pe.wait_ge(tables_landed, 16)
            for t in range(NT):
                transpose_x(0, t)
            ffn(0)
            transpose_x(1, 2)
            transpose_x(1, 3)
            mixer()
            for t in range(NT):
                transpose_x(2, t)
            ffn(1)


NAMES = ("x", "norm_ffn1", "ffn1_gate", "ffn1_up", "ffn1_down", "norm_mix", "w_in", "conv_w", "a_log", "dt_bias",
         "dn_norm", "w_out", "norm_ffn2", "ffn2_gate", "ffn2_up", "ffn2_down", "norm_final")


def kernel(**inputs):
    import concourse.bacc as bacc
    from concourse.bass_utils import run_bass_kernel_spmd

    nc = bacc.Bacc("TRN2", target_bir_lowering=False, num_devices=1)
    arrays = {name: np.ascontiguousarray(inputs[name]) for name in NAMES}
    arrays["table"], arrays["bias"] = shape_tables()
    handles = {n: nc.dram_tensor("in_" + n, a.shape, mybir.dt.from_np(a.dtype), kind="ExternalInput").ap()
               for n, a in arrays.items()}
    result = nc.dram_tensor("out_0", (1, S, D), F32, kind="ExternalOutput").ap()
    decoder_layer(nc, handles, result)
    r = run_bass_kernel_spmd(nc, [{"in_" + n: a for n, a in arrays.items()}], core_ids=[0])
    return r.results[0]["out_0"]
```

```python
from contextlib import ExitStack

import numpy as np

import concourse.bass as bass
from concourse import mybir

F32 = mybir.dt.float32
F32R = mybir.dt.float32r
ALU = mybir.AluOpType
ACT = mybir.ActivationFunctionType
AX_X = mybir.AxisListType.X

P = 128
D, S, F = 1024, 512, 2816
KD, NT, KF = D // P, S // P, F // P
AH, ADH = 8, 64
NH, DH, CH = 4, 128, 64
AW, DW = AH * ADH, NH * DH
COL = dict(aq=0, ak=AW, av=2 * AW, dq=3 * AW, dk=3 * AW + DW, dv=3 * AW + 2 * DW,
           beta=3 * AW + 3 * DW, gate=3 * AW + 3 * DW + 2 * NH)
PATTERNS = ((128, 1), (512, 4), (2048, 16))
CONV = 4
EPS = 1e-6
LEVELS = 6
MASKED = -1e30

RAWS, SPLITS, AHEAD = 2, 4, 2
FFN_SLOTS = 3 * KF
UNITS = [("dk", h) for h in range(NH)] + [("dq", h) for h in range(NH)] + [("dv", h) for h in range(NH)]


SECTIONS = ("dk", "dv", "dq", "gate", "av", "qk0", "qk1", "qk2", "qk3")


def mixer_slots():
    out = []
    for sec in SECTIONS:
        if sec in ("av", "gate"):
            out += [("N", sec, j) for j in range(KD // 2)]
        elif sec[:2] == "qk":
            out += [("T", "aq", int(sec[2])), ("T", "ak", int(sec[2]))]
        else:
            out += [("T", sec, h) for h in range(NH)]
    out += [("O", half, j) for half in range(2) for j in (2, 3, 0)] + [("O", half, 1) for half in range(2)]
    return out


MSLOTS = mixer_slots()
BASE = [0, FFN_SLOTS + len(MSLOTS)]
MBASE = FFN_SLOTS
NSLOTS = 2 * FFN_SLOTS + len(MSLOTS)


PARTS = {
    "fill": "T1.3", "split": "S0.98 G2.24", "conv": "V2.55", "silu": "S1.1", "bdT": "T6.36 V0.99", "bd": "T0.14",
    "g1": "V0.49 S1.47", "g2": "S1.76", "g3": "V0.27", "gc": "T0.45 V0.52", "g4": "S2.07 V0.11", "avs": "S3.04",
    "gates": "S4.76 V3.1", "qk": "S0.31", "t1k": "T0.48 S0.48 V1.06 G1.15", "t1q": "T0.62 S1.13 V1.15 G1.69",
    "t1v": "T0.29 V0.63", "ks": "V0.49 G1.44", "t2": "T0.31 S0.65", "gb": "T0.74 S1.2 V1.51", "qg": "G0.71",
    "ge": "S1", "kk": "T1.13 V1.66 + G1.35", "kq": "T0.74 V0.44", "l1t": "T0.37 V0.87", "W": "T0.55 S0.79 + G0.87",
    "Q": "T0.55 V0.5", "D": "T0.49 S0.55", "uw": "T1.92 S1.55", "chA": "T0.21 V0.41", "chS": "T1.32 V1.45",
    "chO": "T0.65", "o1": "S0.41 V1.22 G1.32", "o2": "V1.43", "outT": "T0.2 S0.27", "aS": "T0.69 V0.39 S0.68",
    "aN": "V0.41", "aT": "T0.45 S0.29", "aV": "T0.38", "aO": "V0.35", "ysplit": "S0.66 V0.69", "last": "T1.72",
}
HANDOVER = 0.2


def unit(sec, h=0):
    return UNITS.index((sec, h))


LAST_IN = len(MSLOTS) - KD - 1


def slot(sec, h=0):
    return next(j for j, (_, s, n) in enumerate(MSLOTS) if (s, n) == (sec, h))


def needs(step):
    kind, i = step[0], step[1] if len(step) > 1 else 0
    if kind == "conv":
        return [("fill", slot(*UNITS[i]), 3)]
    if kind == "silu":
        return [("conv", i)]
    if kind == "t1":
        sec, i = step[1:]
        ready = [("silu", unit("d" + sec, NH - 1))]
        return ready + {"k": [("t2", i - 1), ("g4",), ("uw", i - 2), ("chS", 2 * i - 3)], "q": [("outT", i - 1)],
                        "v": [("uw", i - 1), ("g4",)]}[sec]
    if kind == "ks":
        return [("t1", "k", i)]
    if kind == "t2":
        return [("ks", i)]
    if kind == "gb":
        return [("g4",), ("kk", i - 1), ("chS", 2 * i - 5), ("chO", 2 * i - 5)]
    if kind == "qg":
        return [("gb", i), ("silu", unit("dq", NH - 1))]
    if kind == "ge":
        return [("gb", i)]
    if kind == "kk":
        return [("t2", i), ("ge", i), ("W", i - 1, LEVELS - 1)]
    if kind == "kq":
        return [("t2", i), ("ge", i), ("silu", unit("dq", NH - 1))]
    if kind == "l1t":
        return [("kk", i), ("uw", i - 1)]
    if kind == "W":
        return [("Q", i, step[2] - 1) if step[2] > 1 else ("l1t", i)]
    if kind == "Q":
        return [("W", i, step[2]), ("D", i, step[2] - 1)]
    if kind == "D":
        return [("Q", i, step[2])]
    if kind == "uw":
        return [("Q", i, LEVELS - 1), ("t1", "v", i), ("ks", i), ("chA", 2 * i - 1)]
    if kind == "chA":
        return [("uw", i // 2), ("chS", i - 1), ("chO", i - 2)]
    if kind == "chS":
        return [("chA", i), ("chO", i - 1)]
    if kind == "chO":
        return [("chA", i), ("kq", i // 2), ("qg", i // 2), ("o2", i // 2 - 1)]
    if kind == "o1":
        return [("chO", 2 * i + 1), ("t1", "q", i), ("outT", i - 1)]
    if kind == "o2":
        return [("o1", i), ("gates",)]
    if kind == "outT":
        return [("o2", i)]
    if kind in ("aS", "aN", "aT", "aV"):
        h, q = step[1:]
        m = NT * h + q

        def key(kind, m):
            return kind, m // NT, m % NT

        return {"aS": [("qk", h // 2, 1), key("aT", m - 2)], "aN": [key("aS", m)],
                "aT": [key("aN", m), key("aV", m - 2)],
                "aV": [key("aT", m), ("avs",), ("gates",), ("aO", h // 2 - 1)]}[kind]
    if kind == "aO":
        return [("aV", 2 * i + 1, NT - 1)]
    if kind == "qk":
        return [("aS", 2 * i - 3, NT - 1)]
    if kind == "ysplit":
        return [("outT", NT - 1) if i >= AW // P else ("aO", i), ("fill", LAST_IN, 3)]
    if kind == "fill" and MSLOTS[i][0] == "O":
        n = MSLOTS[i][2]
        ends = [("outT", NT - 1), ("aO", AH // 2 - 1)] if MSLOTS[i][1] else []
        return [("ysplit", 2 * n + 1), ("o2", NT - 1)] + ends
    return []


ROTATING = ("bdT", "bd", "gc", "t1", "t2", "gb", "kk", "kq", "l1t", "W", "Q", "D", "chA", "chS", "outT", "aS", "aT")


def weave(streams):
    everything = {step for stream in streams for step in stream}
    at, done, free, out, banks = [0] * len(streams), {}, dict.fromkeys("TSVG", 0.0), [], [0.0] * 3

    def run(parts, t):
        for part in parts.split():
            t = max(t, free[part[0]]) + float(part[1:])
            free[part[0]] = t
            t += HANDOVER
        return t

    while len(out) < len(everything):
        best = None
        for n, stream in enumerate(streams):
            if at[n] < len(stream):
                step = stream[at[n]]
                parts = PARTS[step[0] + step[1] if step[0] == "t1" else step[0]]
                before = [s for s in needs(step) if s in everything]
                if all(s in done for s in before):
                    ready = max([free[parts[0]]] + [done[s] for s in before])
                    if step[0] in ROTATING:
                        ready = max(ready, banks[-3])
                    if best is None or ready < best[0]:
                        best = (ready, n, parts)
        ready, n, parts = best
        step = streams[n][at[n]]
        at[n] += 1
        chain, _, beside = parts.partition("+")
        if step[0][0] == "a" and len(step) == 3:
            chain = " ".join(p[0] + str(float(p[1:]) * (step[2] + 1.5) / 3) for p in chain.split())
        done[step] = run(chain, ready)
        run(beside, ready)
        if step[0] == "fill" and step[2] == 0:
            run(PARTS["split"], ready)
        if step[0] in ROTATING:
            banks.append(done[step])
        out.append(step)
    return out


def mixer_order():
    def fill(j):
        return [("fill", j, q) for q in range(4)]

    gate_math = {0: [("bdT",)], 1: [("bd",), ("g1",)], 2: [("g2",), ("g3",)], 3: [("gc",), ("g4",)]}
    flow = []
    for j, (what, sec, n) in enumerate(MSLOTS):
        if what == "T":
            flow += fill(j)
            flow += [("conv", UNITS.index((sec, n)))] if sec[0] == "d" else [("qk", n, int(sec == "ak"))]
        elif what == "N":
            flow += fill(j)
            if n == KD // 2 - 1:
                flow.append({"av": ("avs",), "gate": ("gates",)}[sec])
        elif j in (LAST_IN + 3, LAST_IN + 4):
            k = 2 * (j - LAST_IN - 3)
            flow += [("ysplit", k), ("ysplit", k + 1)] + fill(j)
        elif j < len(MSLOTS) - 2:
            flow += fill(j)
        if j == LAST_IN:
            flow += [("ysplit", k) for k in range(AW // P, KD)]
        flow += gate_math.get(j, [])
        if j >= 1 and MSLOTS[j - 1][1:] in UNITS:
            flow.append(("silu", UNITS.index(MSLOTS[j - 1][1:])))
    flow += [("last", t) for t in range(NT)]

    tile, ahead, asides, chunk, output, attention = [], [], [], [], [], []
    for i in range(NT):
        ahead += [("t1", "k", i), ("ks", i), ("t2", i), ("gb", i), ("ge", i)]
        asides += [("qg", i), ("kq", i)]
        tile += [("kk", i), ("l1t", i)]
        for lev in range(1, LEVELS):
            tile += [("W", i, lev), ("Q", i, lev)] + [("D", i, lev)] * (lev < LEVELS - 1)
        tile.append(("uw", i))
        for n in (2 * i, 2 * i + 1):
            chunk += [("chA", n), ("chS", n), ("chO", n)]
        output += [("t1", "q", i), ("o1", i), ("o2", i), ("outT", i)]
    values = [("t1", "v", i) for i in range(NT)]
    heads = [(h, q) for h in range(AH) for q in range(NT)]
    scores, scaled, turned = ([(kind, *m) for m in heads] for kind in ("aS", "aN", "aT"))
    for h, q in heads:
        attention.append(("aV", h, q))
        if h % 2 == 1 and q == NT - 1:
            attention.append(("aO", h // 2))
    return weave([chunk, scaled, output, ahead, attention, turned, scores, tile, values, asides, flow])


ORDER = mixer_order()


def plan_banks():
    use, count, up = {}, [0] * 8, []

    def take(key, bank):
        count[bank] += 1
        use[key] = (bank, count[bank])

    def norm(n):
        for t in range(NT):
            for half in range(2):
                take(("xT", n, t, half), 2 * t + half)

    def ffn(f):
        up.append(list(count[:4]))
        for b in range(4):
            count[b] += KF // 2
        for t in range(NT):
            for half in range(2):
                take(("y", f, t, half), 2 * t + half)

    norm(0)
    ffn(0)
    norm(1)
    ring, held = [4, 5, 6], {}

    def rotate(key):
        b = next(b for b in ring if b not in held.values())
        ring.remove(b)
        ring.append(b)
        take(key, b)

    rotate(("cw",))
    for step in ORDER:
        kind = step[0]
        if kind == "fill" and step[2] == 0:
            what, sec, j = MSLOTS[step[1]]
            if what == "T":
                take(("T", step[1]), step[1] % 2)
            elif what == "N" and j == 0:
                for t in range(NT):
                    take(("N", sec, t), t)
            elif what == "O" and j == 2:
                if sec == 0:
                    ring.remove(2)
                for t in range(NT):
                    take(("o", sec, t), ((0, 1, 2, 7), (3, 4, 5, 6))[sec][t])
        elif kind in ROTATING:
            rotate(step)
            if step[:2] == ("t1", "k"):
                held[step[2]] = use[step][0]
        elif kind == "ks":
            del held[step[1]]
        elif kind == ("gates" if SECTIONS.index("gate") > SECTIONS.index("av") else "avs"):
            ring.insert(0, 2)
        elif kind == "uw":
            rotate(("u", step[1]))
            rotate(("w", step[1]))
        elif kind == "chO" and step[1] % 2 == 0:
            take(("PO", step[1] // 2), 7)
        elif kind == "aV" and step[1] % 2 == 0 and step[2] == 0:
            take(("O", step[1] // 2), 3)
    norm(2)
    ffn(1)
    return use, up


USE, UP_BASE = plan_banks()


def shape_tables():
    r = np.arange(P)
    row, col = r[:, None], r[None, :]
    chunk = row // CH == col // CH
    parts = [np.eye(P), chunk & (row <= col), chunk,
             np.where(chunk & (col <= row), 0.0, MASKED), np.where(chunk & (row <= col), 0.0, MASKED)]
    for lev in range(LEVELS):
        b = 1 << lev
        parts.append((row // (2 * b) == col // (2 * b)) & (row // b % 2 == 1) & (col // b % 2 == 0))
    table = np.concatenate([np.asarray(x, np.float32) for x in parts], axis=1)
    dist = row + (S - P) - np.arange(S)[None, :]
    times = sum(((dist >= 0) & (dist % d == 0) & (dist // d <= w // d)).astype(np.int64) for w, d in PATTERNS)
    base = np.where(times > 0, np.log(np.maximum(times, 1)), MASKED)
    slopes = [2.0 ** (-8.0 * (i + 1) / AH) for i in range(AH)]
    bias = np.stack([(base - s * dist) * ADH ** 0.5 for s in slopes])
    return table, bias.astype(np.float32)


def decoder_layer(nc, A, out):
    ctx = ExitStack()
    with ctx:
        start = (nc.sbuf_base + 31) // 32 * 32
        at = [start]

        def sb(name, shape, dt=F32):
            n = 4 * int(np.prod(shape[1:]))
            h = nc.alloc_sbuf_tensor_at(name, shape, dt, offset=at[0])
            at[0] += (n + 31) // 32 * 32
            return h

        w_raw = sb("w_raw", [P, RAWS, 1024])
        w_hi = sb("w_hi", [P, SPLITS, 1024], F32R)
        w_lo = sb("w_lo", [P, SPLITS, 1024], F32R)
        xT_hi = sb("xT_hi", [P, KD, S], F32R)
        xT_lo = sb("xT_lo", [P, KD, S], F32R)
        table = sb("table", [P, 5 + LEVELS, P])
        gain = sb("gain", [P, D])
        ssq = sb("ssq", [P, 4 * NT + 1])
        rstd = sb("rstd", [P, 4 * NT])
        minus_half = sb("minus_half", [P, 1])
        conv_w = sb("conv_w", [P, CONV * len(UNITS)])
        conv_rows = sb("conv_rows", [CONV * len(UNITS), P])
        wbd = sb("wbd", [P, KD, 2 * NH])
        wbd_hi = sb("wbd_hi", [P, KD, 2 * NH], F32R)
        wbd_lo = sb("wbd_lo", [P, KD, 2 * NH], F32R)
        dtb = sb("dtb", [P, NH])
        alog = sb("alog", [P, NH])
        dnn = sb("dnn", [P, DH])
        gt = {n: sb("g_" + n, [P, NT, NH]) for n in
              ("z", "zn", "mz", "e", "ln", "g", "eb", "beta", "eg", "ekd", "beg", "gd")}
        gcum = sb("gcum", [P, 2, NT, NH])
        expa = sb("expa", [P, NH])
        ss_qk = sb("ss_qk", [P, 2, NT, NH])
        rn_qk = sb("rn_qk", [P, 2, NT, NH])
        egl = sb("egl", [P, 3, NH, 2])
        ss_o = sb("ss_o", [P, NT, NH])
        ms_o = sb("ms_o", [P, NT, NH])
        rs_o = sb("rs_o", [P, NT, NH])
        r2_q = sb("r2_q", [P, NT, NH])
        nmax = sb("nmax", [P, AH * NT])
        den = sb("den", [P, AH * NT])
        rden = sb("rden", [P, AH * NT])
        arena = at[0]
        x = sb("x", [P, NT, D])
        after_x = at[0]
        hT = sb("hT", [P, KF, S])
        h_hi = sb("h_hi", [P, 2, S], F32R)
        h_lo = sb("h_lo", [P, 2, S], F32R)
        sg = sb("sg", [P, 2, S])
        xs = sb("xs", [P, NT, D])
        assert at[0] <= nc.sbuf_usable_end
        at[0] = arena
        av = sb("av", [P, NT, AW])
        gs = sb("gs", [P, NT, DW])
        assert at[0] <= after_x
        sil = sb("sil", [P, len(UNITS), S])
        kn = sb("kn", [P, NH, DH])
        vb = sb("vb", [P, NH, DH])
        kbeg = sb("kbeg", [P, 2, NH, DH])
        kdec = sb("kdec", [P, 2, NH, DH])
        qgT = sb("qgT", [P, 3, NH, P])
        dec = sb("dec", [P, NH, P])
        Am = sb("Am", [P, NH, P])
        Lm = sb("Lm", [P, 2, NH, P])
        Di = sb("Di", [P, NH, P])
        DiT = sb("DiT", [P, NH, P])
        Wm = sb("Wm", [P, NH, P])
        attnT = sb("attnT", [P, 3, NH, P])
        u = sb("u", [P, NH, DH])
        wT = sb("wT", [P, NH, P])
        vnew = sb("vnew", [P, NH, DH])
        St = sb("St", [P, 2, NH, DH])
        y = sb("y", [P, NH, DH])
        qk = sb("qk", [P, 2, 2, S])
        pr = sb("pr", [P, 2, S])
        ab = sb("ab", [P, 2, S])
        yT = sb("yT", [P, KD, S])
        assert at[0] <= nc.sbuf_usable_end, at[0] - nc.sbuf_usable_end
        pT = gain[:].rearrange("p (b n) -> p b n", b=2)
        bdT = pr[0:2 * NH, 0, :]
        x_kept = nc.dram_tensor("x_kept", [S, D], F32, kind="Internal").ap().rearrange("(t p) d -> p t d", p=P)

        ident, upto, same = table[:, 0, :], table[:, 1, :], table[:, 2, :]
        neg, negT = table[:, 3, :], table[:, 4, :]
        bank = [ctx.enter_context(nc.psum_tensor(f"bank{b}", [P, 512], F32)) for b in range(8)]

        def per_head(ap):
            return ap.rearrange("p (h c) -> p h c", h=NH)

        def blocks(ap, c):
            r = slice(c * CH, (c + 1) * CH)
            return ap[r, :, r]

        def over(ap, n=P):
            return ap.unsqueeze(2).broadcast_to([P, NH, n])

        def sem(name):
            return ctx.enter_context(nc.semaphore(name))

        filled = [sem(f"filled{b}") for b in range(8)]
        drained = [sem(f"drained{b}") for b in range(8)]
        raw_landed = [sem(f"raw_landed{r}") for r in range(RAWS)]
        hi_done = sem("hi_done")
        split_done = sem("split_done")
        slots_begun = sem("slots_begun")
        x_landed = [sem(f"x_landed{t}") for t in range(NT)]
        ident_landed = sem("ident_landed")
        tables_landed = sem("tables_landed")
        small_landed = sem("small_landed")
        bias_landed = [sem(f"bias_landed{b}") for b in range(2)]
        gain_landed = sem("gain_landed")
        x_spilled = sem("x_spilled")
        x_back = sem("x_back")
        stored = sem("stored")
        half_set = sem("half_set")
        sq_done = sem("sq_done")
        rstd_done = sem("rstd_done")
        xs_done = sem("xs_done")
        xT_rounded = sem("xT_rounded")
        h_rounded = sem("h_rounded")
        h_split = sem("h_split")
        small_split = sem("small_split")
        gate_math = sem("gate_math")
        silu_done = sem("silu_done")
        norm_squared = {c: sem("norm_squared_" + c) for c in "kq"}
        k_summed = sem("k_summed")
        k_rooted = sem("k_rooted")
        q_rooted = sem("q_rooted")
        k_scaled = sem("k_scaled")
        q_decayed = sem("q_decayed")
        bcast_exp = sem("bcast_exp")
        dec_done = sem("dec_done")
        L0_done = sem("L0_done")
        L_done = sem("L_done")
        Di_done = sem("Di_done")
        state_zero = sem("state_zero")
        o_squared = sem("o_squared")
        o_summed = sem("o_summed")
        o_rooted = sem("o_rooted")
        y_done = sem("y_done")
        gate_silu = sem("gate_silu")
        gate_gained = sem("gate_gained")
        exp_done = sem("exp_done")
        probs_done = sem("probs_done")
        y_rounded = sem("y_rounded")
        y_split = sem("y_split")
        dve_own = sem("dve_own")
        act_own = sem("act_own")
        pool_own = sem("pool_own")

        def open_bank(eng, key):
            b, n = USE[key]
            if n > 1:
                eng.wait_ge(drained[b], n - 1)
            return bank[b]

        def wait_filled(eng, key):
            b, n = USE[key]
            eng.wait_ge(filled[b], n)
            return bank[b]

        def wait_drained(eng, key):
            b, n = USE[key]
            eng.wait_ge(drained[b], n)

        def full(key):
            return filled[USE[key][0]]

        def drain(key):
            return drained[USE[key][0]]

        def wait_silu(eng, sec):
            done = [s for s in ORDER if s[0] == "silu"]
            eng.wait_ge(silu_done, 1 + done.index(("silu", unit(sec, NH - 1))))

        def wait_added(eng, r, t):
            for half in range(2):
                wait_drained(eng, ("o", half, t) if r == 1 else ("y", r // 2, t, half))

        w_in = A["w_in"][0].rearrange("(k p) n -> p k n", p=P)
        w_out = A["w_out"][0].rearrange("(k p) n -> p k n", p=P)
        gates_in = [A[n][0].rearrange("(k p) n -> p k n", p=P) for n in ("ffn1_gate", "ffn2_gate")]
        ups_in = [A[n][0].rearrange("(k p) n -> p k n", p=P) for n in ("ffn1_up", "ffn2_up")]
        downs_in = [A[n][0] for n in ("ffn1_down", "ffn2_down")]
        x_in = A["x"][0].rearrange("(t p) d -> p t d", p=P)
        out_v = out[0].rearrange("(t p) d -> p t d", p=P)
        gains = [A["norm_ffn1"], A["norm_mix"], A["norm_ffn2"], A["norm_final"]]

        block = ctx.enter_context(nc.Block())

        @block.sync
        def _(sp):
            def load(w, ring, src, split):
                sp.wait_ge(split_done, w + 1)
                dst = w_raw[:, ring, :]
                if split > 1:
                    dst = dst.rearrange("p (k n) -> p k n", k=split)
                sp.dma_start(dst, src).then_inc(raw_landed[ring], 16)

            def load_gain(n):
                if n:
                    sp.wait_ge(xs_done, NT * n)
                src = gains[n][0:1, :] if n < 3 else gains[n].rearrange("(a d) -> a d", a=1)
                sp.dma_start(gain[:], src.broadcast_to([P, D])).then_inc(gain_landed, 16)

            def ffn_stream(f):
                for c in range(1 - f, 2):
                    for g, src in enumerate((gates_in[f], ups_in[f])):
                        load(BASE[f] + 2 * c + g, g, src[:, :, c * P:(c + 1) * P], KD)
                load_gain(2 * f + 1)
                with sp.Fori(1, KF // 2) as i:
                    for c in range(2):
                        for g, src in enumerate((gates_in[f], ups_in[f])):
                            load(BASE[f] + 4 * i + 2 * c + g, g,
                                 src[:, :, bass.ds(i * 256 + c * 128, P)], KD)
                base = BASE[f] + 2 * KF
                with sp.Fori(0, KF // 2) as i:
                    for c in range(2):
                        load(base + 2 * i + c, c, downs_in[f][bass.ds(i * 256 + c * 128, P), :], 1)

            tables_in = A["table"].rearrange("p (m n) -> p m n", n=P)
            for t in range(NT):
                sp.dma_start(x[:, t, :], x_in[:, t, :]).then_inc(x_landed[t], 16)
                if t == 0:
                    load_gain(0)
                    sp.dma_start(table[:, 0:1, :], tables_in[:, 0:1, :]).then_inc(ident_landed, 16)
                if t == 1:
                    for g, src in enumerate((gates_in[0], ups_in[0])):
                        load(g, g, src[:, :, 0:P], KD)
            sp.dma_start(table[:, 1:, :], tables_in[:, 1:, :]).then_inc(tables_landed, 16)

            ffn_stream(0)
            for j, (what, sec, n) in enumerate(MSLOTS):
                if j == 2:
                    sp.wait_ge(xs_done, 2 * NT)
                    sp.dma_start(x_kept, x[:]).then_inc(x_spilled, 16)
                if j == len(MSLOTS) - 1:
                    wait_filled(sp, ("O", AH // 2 - 1))
                    sp.wait_ge(y_done, NT)
                    sp.wait_ge(x_spilled, 16)
                    sp.dma_start(x[:], x_kept).then_inc(x_back, 16)
                    load_gain(2)
                w = MBASE + j
                if what == "T":
                    load(w, w % RAWS, w_in[:, :, COL[sec] + n * P:COL[sec] + (n + 1) * P], KD)
                elif what == "N":
                    load(w, w % RAWS, w_in[:, 2 * n:2 * n + 2, COL[sec]:COL[sec] + 512], 2)
                else:
                    load(w, w % RAWS, w_out[:, 2 * n:2 * n + 2, sec * 512:(sec + 1) * 512], 2)
            ffn_stream(1)
            for t in range(NT - 1):
                sp.wait_ge(xs_done, 3 * NT + t + 1)
                sp.dma_start(out_v[:, t, :], xs[:, t, :]).then_inc(stored, 16)
            for half in range(2):
                sp.wait_ge(xs_done, 4 * NT + half)
                part = slice(half * 512, half * 512 + 512)
                sp.dma_start(out_v[:, NT - 1, part], xs[:, NT - 1, part]).then_inc(stored, 16)
            sp.wait_ge(stored, 16 * (NT + 1))

        @block.scalar
        def _(act):
            own = [0]

            def link(ins):
                own[0] += 1
                ins.then_inc(act_own, 1)
                act.wait_ge(act_own, own[0])

            def round_slot(w, ring, waits=True):
                act.wait_ge(raw_landed[ring % RAWS], 16 * (w // RAWS) + 16)
                if waits:
                    act.wait_ge(slots_begun, w - 2)
                act.activation(w_hi[:, ring, :], w_raw[:, ring % RAWS, :], ACT.Copy).then_inc(hi_done, 1)

            def round_looped(base, i, per, off):
                w0 = base + off
                act.wait_ge(raw_landed[w0 % RAWS], 16 * (per // RAWS) * i + 16 * (w0 // RAWS) + 16)
                act.wait_ge(slots_begun, per * i + (w0 - 2))
                act.activation(w_hi[:, w0 % SPLITS, :], w_raw[:, w0 % RAWS, :], ACT.Copy).then_inc(hi_done, 1)

            def square(n, t):
                if n == 0:
                    act.wait_ge(x_landed[t], 16)
                else:
                    wait_added(act, n - 1, t)
                act.activation(xs[:, t, :], x[:, t, :], ACT.Square,
                               accum_out=ssq[:, 4 * n + t:4 * n + t + 1]).then_inc(sq_done, 1)

            def norm(n):
                square(n, 0)
                square(n, 1)
                for t in (0, 1):
                    round_x(n, t)
                    if n == 0:
                        round_slot(t, t, waits=False)
                    square(n, t + 2)
                round_x(n, 2)
                round_x(n, 3)

            def round_x(n, t):
                for half in range(2):
                    ps = wait_filled(act, ("xT", n, t, half))
                    act.activation(xT_hi[:, 4 * half:4 * half + 4, t * P:(t + 1) * P],
                                   per_head(ps[:]), ACT.Copy).then_inc(xT_rounded, 1)

            def ffn(f):
                b, n = BASE[f], UP_BASE[f]
                with act.Fori(0, KF // 2) as i:
                    for c in range(2):
                        round_looped(b, i, 4, 2 * c + 2)
                        round_looped(b, i, 4, 2 * c + 3)
                        act.wait_ge(filled[2 * c], i + n[2 * c] + 1)
                        act.wait_ge(drained[2 * c + 1], i + n[2 * c + 1])
                        act.activation(sg[:, c, :], bank[2 * c][:], ACT.Silu).then_inc(drained[2 * c], 1)
                act.wait_ge(drained[1], n[1] + 1)
                act.activation(h_hi[:, 0, :], hT[:, 0, :], ACT.Copy).then_inc(h_rounded, 1)
                act.wait_ge(drained[3], n[3] + KF // 2)

                b = BASE[f] + 2 * KF

                for kt in range(2):
                    round_slot(b + kt + AHEAD, (b + kt + AHEAD) % SPLITS)
                    act.wait_ge(slots_begun, b + kt + 1)
                    act.activation(h_hi[:, (kt + 1) % 2, :], hT[:, kt + 1, :], ACT.Copy).then_inc(h_rounded, 1)
                with act.Fori(0, 4) as i:
                    for c in range(4):
                        round_looped(b, i, 4, 2 + c + AHEAD)
                        act.wait_ge(slots_begun, 4 * i + (b + 2 + c + 1))
                        act.activation(h_hi[:, (3 + c) % 2, :],
                                       hT[:].rearrange("p k n -> p (k n)")[:, bass.ds(i * (4 * S) + (3 + c) * S, S)],
                                       ACT.Copy).then_inc(h_rounded, 1)
                for kt in range(18, KF):
                    if b + kt + AHEAD < NSLOTS:
                        round_slot(b + kt + AHEAD, (b + kt + AHEAD) % SPLITS)
                    if kt + 1 < KF:
                        act.wait_ge(slots_begun, b + kt + 1)
                        act.activation(h_hi[:, (kt + 1) % 2, :], hT[:, kt + 1, :], ACT.Copy).then_inc(h_rounded, 1)

            def mixer():
                wait_filled(act, ("xT", 1, NT - 1, 1))
                for h in range(2):
                    act.dma_start(ab[:, h, :], A["bias"][h]).then_inc(bias_landed[h], 16)
                act.wait_ge(small_landed, 16 * 5)
                act.activation(wbd_hi[:], wbd[:], ACT.Copy).then_inc(small_split, 1)
                for step in ORDER:
                    kind = step[0]
                    if kind == "fill":
                        w = MBASE + step[1] + AHEAD
                        if step[2] == 0:
                            round_slot(w, w % SPLITS)
                    elif kind == "last" and step[1] < AHEAD:
                        w = BASE[1] + step[1]
                        round_slot(w, w % SPLITS)
                    elif kind == "silu":
                        wait_drained(act, ("T", slot(*UNITS[step[1]])))
                        act.activation(sil[:, step[1], :], sil[:, step[1], :], ACT.Silu).then_inc(silu_done, 1)
                    elif kind == "avs":
                        act.wait_ge(x_spilled, 16)
                        for t in range(NT):
                            ps = wait_filled(act, ("N", "av", t))
                            act.activation(av[:, t, :], ps[:], ACT.Copy).then_inc(drain(("N", "av", t)), 1)
                    elif kind == "gates":
                        act.wait_ge(x_spilled, 16)
                        for t in range(NT):
                            ps = wait_filled(act, ("N", "gate", t))
                            act.activation(gs[:, t, :], ps[:], ACT.Silu).then_inc(drain(("N", "gate", t)), 1)
                    elif kind == "qk":
                        key = ("T", slot(("aq", "ak")[step[2]], step[1]))
                        ps = wait_filled(act, key)
                        act.activation(qk[:, step[1] % 2, step[2], :], ps[:], ACT.Copy).then_inc(drain(key), 1)
                    elif kind == "g1":
                        act.wait_ge(gate_math, 1)
                        ps = bank[USE[("bd",)][0]]
                        act.activation(gt["eb"][:], ps[:, 0:NT * 2 * NH].rearrange("p (t n) -> p t n", t=NT)[:, :, 0:NH],
                                       ACT.Exp, scale=-1.0).then_inc(drain(("bd",)), 1)
                        act.activation(expa[:], alog[:], ACT.Exp)
                    elif kind == "g2":
                        act.wait_ge(gate_math, 2)
                        link(act.activation(gt["e"][:], gt["e"][:], ACT.Exp))
                        act.activation(gt["ln"][:], gt["e"][:], ACT.Ln, bias=1.0).then_inc(gate_math, 1)
                    elif kind == "g4":
                        act.wait_ge(gate_math, 5)
                        act.activation(gt["eg"][:], gcum[:, 0, :, :], ACT.Exp)
                        act.activation(gt["ekd"][:], gt["gd"][:], ACT.Exp).then_inc(gate_math, 1)
                    elif kind == "t1" and step[1] != "v":
                        c, i = step[1:]
                        if c == "k" and i >= 1:
                            act.wait_ge(k_scaled, 2 * i)
                            wait_filled(act, ("t2", i - 1))
                        if c == "q" and i >= 1:
                            wait_filled(act, ("outT", i - 1))
                        ps = wait_filled(act, step)
                        act.activation((kn if c == "k" else y)[:], per_head(ps[:]), ACT.Square)\
                           .then_inc(norm_squared[c], 1)
                    elif kind == "t2":
                        i = step[1]
                        first = unit("dk")
                        ps = wait_filled(act, step)
                        act.activation(sil[:, first:first + NH, i * P:(i + 1) * P], per_head(ps[:]), ACT.Copy)\
                           .then_inc(drain(step), 1)
                    elif kind == "gb":
                        i = step[1]
                        ps = wait_filled(act, step)
                        if i >= 3:
                            wait_filled(act, ("PO", i - 3))
                            wait_drained(act, ("chS", 2 * i - 5))
                        act.activation(egl[:, i % 3, :, :],
                                       ps[:].rearrange("p (h c j) -> p h c j", h=NH, c=2)[:, :, :, CH - 1], ACT.Exp)
                        act.activation(qgT[:, i % 3, :, :], per_head(ps[:]), ACT.Exp).then_inc(bcast_exp, 1)
                    elif kind == "ge":
                        i = step[1]
                        wait_drained(act, ("gb", i))
                        act.activation(dec[:], dec[:], ACT.Exp, scale=-1.0)
                        decT = attnT[:, i % 3, :, :]
                        act.activation(decT, decT, ACT.Exp).then_inc(dec_done, 1)
                    elif kind == "W":
                        ps = wait_filled(act, step)
                        act.activation(blocks(Wm, 0), blocks(per_head(ps[:]), 0), ACT.Copy)
                        act.activation(blocks(Wm, 1), blocks(per_head(ps[:]), 1), ACT.Copy).then_inc(drain(step), 1)
                    elif kind == "D":
                        ps = wait_filled(act, step)
                        act.activation(Di[:], per_head(ps[:]), ACT.Copy).then_inc(drain(step), 1)
                    elif kind == "uw":
                        i = step[1]
                        if i >= 1:
                            wait_drained(act, ("chA", 2 * i - 1))
                        ps = wait_filled(act, ("u", i))
                        act.activation(u[:], per_head(ps[:]), ACT.Copy).then_inc(drain(("u", i)), 1)
                        ps = wait_filled(act, ("w", i))
                        act.activation(wT[:], per_head(ps[:]), ACT.Copy).then_inc(drain(("w", i)), 1)
                    elif kind == "o1":
                        i = step[1]
                        wait_drained(act, ("t1", "q", i))
                        ps = wait_filled(act, ("PO", i))
                        act.activation(y[:], per_head(ps[:]), ACT.Square).then_inc(o_squared, 1)
                    elif kind == "outT":
                        i = step[1]
                        ps = wait_filled(act, step)
                        act.activation(yT[:, AW // P:, i * P:(i + 1) * P], per_head(ps[:]), ACT.Copy)\
                           .then_inc(drain(step), 1)
                    elif kind == "aS":
                        h, q = step[1:]
                        m, n = NT * h + q, (q + 1) * P
                        wait_drained(act, step)
                        act.activation(pr[:, m % 2, 0:n], pr[:, m % 2, 0:n], ACT.Exp, scale=-1.0,
                                       bias=nmax[:, m:m + 1], accum_out=den[:, m:m + 1]).then_inc(exp_done, 1)
                        if q == NT - 1 and h + 2 < AH:
                            act.dma_start(ab[:, h % 2, :], A["bias"][h + 2]).then_inc(bias_landed[h % 2], 16)
                    elif kind == "aT":
                        ps = wait_filled(act, step)
                        n = (step[2] + 1) * P
                        act.activation(pT[:, step[2] % 2, 0:n], ps[:, 0:n], ACT.Copy).then_inc(drain(step), 1)
                    elif kind == "ysplit":
                        k = step[1]
                        if k == 4:
                            wait_filled(act, ("T", LAST_IN))
                        wait_drained(act, ("outT", NT - 1) if k >= 4 else ("O", k))
                        act.activation(xT_hi[:, k, :], yT[:, k, :], ACT.Copy).then_inc(y_rounded, 1)

            norm(0)
            act.dma_start(wbd[:], w_in[:, :, COL["beta"]:COL["beta"] + 2 * NH]).then_inc(small_landed, 16)
            act.dma_start(conv_rows[:], A["conv_w"][0].rearrange("j (u p) -> (j u) p", p=P)).then_inc(small_landed, 16)
            act.dma_start(dtb[:], A["dt_bias"][0:1, :].broadcast_to([P, NH])).then_inc(small_landed, 16)
            act.dma_start(alog[:], A["a_log"][0:1, :].broadcast_to([P, NH])).then_inc(small_landed, 16)
            act.dma_start(dnn[:], A["dn_norm"][0:1, :].broadcast_to([P, DH])).then_inc(small_landed, 16)
            ffn(0)
            norm(1)
            mixer()
            norm(2)
            ffn(1)
            for t in range(NT - 1):
                square(3, t)
            for half in range(2):
                wait_drained(act, ("y", 1, NT - 1, half))
                part = slice(half * 512, half * 512 + 512)
                act.activation(xs[:, NT - 1, part], x[:, NT - 1, part], ACT.Square,
                               accum_out=ssq[:, 4 * NT - 1 + half:4 * NT + half]).then_inc(sq_done, 1)

        @block.vector
        def _(dve):
            own = [0]

            def link(ins):
                own[0] += 1
                ins.then_inc(dve_own, 1)
                dve.wait_ge(dve_own, own[0])

            def rest_of_slot(w, ring):
                dve.wait_ge(hi_done, w + 1)
                dve.tensor_tensor(w_lo[:, ring, :], w_raw[:, ring % RAWS, :], w_hi[:, ring, :].bitcast(F32),
                                  ALU.subtract).then_inc(split_done, 1)

            def scale_x(n, t):
                if t == 0:
                    dve.wait_ge(gain_landed, 16 * (n + 1))
                dve.wait_ge(rstd_done, NT * n + t + 1)
                dve.scalar_tensor_tensor(out=xs[:, t, :], in0=x[:, t, :], scalar=rstd[:, 4 * n + t:4 * n + t + 1],
                                         in1=gain[:], op0=ALU.mult, op1=ALU.mult).then_inc(xs_done, 1)

            def rest_of_x(n, t):
                for half in range(2):
                    key = ("xT", n, t, half)
                    dve.wait_ge(xT_rounded, 8 * n + 2 * t + half + 1)
                    dve.tensor_tensor(xT_lo[:, 4 * half:4 * half + 4, t * P:(t + 1) * P],
                                      per_head(bank[USE[key][0]][:]),
                                      xT_hi[:, 4 * half:4 * half + 4, t * P:(t + 1) * P].bitcast(F32),
                                      ALU.subtract).then_inc(drain(key), 1)

            def norm(n, add=None):
                if add is not None:
                    add(0)
                    add(1)
                scale_x(n, 0)
                scale_x(n, 1)
                if add is not None:
                    add(2)
                for t in (0, 1):
                    rest_of_x(n, t)
                    if n == 0:
                        rest_of_slot(t, t)
                if add is not None:
                    add(3)
                scale_x(n, 2)
                scale_x(n, 3)
                rest_of_x(n, 2)
                rest_of_x(n, 3)

            def add_ffn(f, t):
                for half in range(2):
                    key = ("y", f, t, half)
                    ps = wait_filled(dve, key)
                    part = x[:, t, half * 512:(half + 1) * 512]
                    dve.scalar_tensor_tensor(out=part, in0=ps[:], scalar=0.5, in1=part,
                                             op0=ALU.mult, op1=ALU.add).then_inc(drain(key), 1)

            def add_mixer(t):
                for half in range(2):
                    key = ("o", half, t)
                    ps = wait_filled(dve, key)
                    part = x[:, t, half * 512:(half + 1) * 512]
                    dve.tensor_tensor(part, part, ps[:], ALU.add).then_inc(drain(key), 1)

            def ffn(f):
                b, n = BASE[f], UP_BASE[f]
                dve.wait_ge(split_done, b + AHEAD + RAWS)
                with dve.Fori(0, KF // 2) as i:
                    for c in range(2):
                        rest_of_slot(4 * i + (b + 2 * c + 2), (b + 2 * c + 2) % SPLITS)
                        rest_of_slot(4 * i + (b + 2 * c + 3), (b + 2 * c + 3) % SPLITS)
                        dve.wait_ge(drained[2 * c], i + n[2 * c] + 1)
                        dve.wait_ge(filled[2 * c + 1], i + n[2 * c + 1] + 1)
                        dve.tensor_tensor(hT[:].rearrange("p k n -> p (k n)")[:, bass.ds(i * (2 * S) + c * S, S)],
                                          sg[:, c, :], bank[2 * c + 1][:], ALU.mult).then_inc(drained[2 * c + 1], 1)
                h0 = f * KF
                dve.wait_ge(drained[3], n[3] + KF // 2)
                b = BASE[f] + 2 * KF

                def rest_of_h(value, k, src):
                    dve.wait_ge(h_rounded, value)
                    dve.tensor_tensor(h_lo[:, k % 2, :], src, h_hi[:, k % 2, :].bitcast(F32), ALU.subtract)\
                       .then_inc(h_split, 1)

                for kt in range(2):
                    rest_of_slot(b + kt + AHEAD, (b + kt + AHEAD) % SPLITS)
                    rest_of_h(h0 + kt + 2, kt + 1, hT[:, kt + 1, :])
                with dve.Fori(0, 4) as i:
                    for c in range(4):
                        rest_of_slot(4 * i + (b + 2 + c + AHEAD), (b + 2 + c + AHEAD) % SPLITS)
                        rest_of_h(4 * i + (h0 + 2 + c + 2), 3 + c,
                                  hT[:].rearrange("p k n -> p (k n)")[:, bass.ds(i * (4 * S) + (3 + c) * S, S)])
                for kt in range(18, KF):
                    if b + kt + AHEAD < NSLOTS:
                        rest_of_slot(b + kt + AHEAD, (b + kt + AHEAD) % SPLITS)
                    if kt + 1 < KF:
                        rest_of_h(h0 + kt + 2, kt + 1, hT[:, kt + 1, :])

            def mixer():
                dve.wait_ge(tables_landed, 16)
                dve.wait_ge(small_split, 1)
                dve.tensor_tensor(wbd_lo[:], wbd[:], wbd_hi[:].bitcast(F32), ALU.subtract).then_inc(small_split, 1)
                ps = wait_filled(dve, ("cw",))
                dve.tensor_copy(conv_w[:], ps[:, 0:CONV * len(UNITS)]).then_inc(drain(("cw",)), 1)
                wide = [P, NT, NH]
                for step in ORDER:
                    kind = step[0]
                    if kind == "conv":
                        j = step[1]
                        sec, h = UNITS[j]
                        unit = {"dq": 0, "dk": NH, "dv": 2 * NH}[sec] + h
                        ps = wait_filled(dve, ("T", slot(*UNITS[j])))
                        w = [conv_w[:, c * len(UNITS) + unit:c * len(UNITS) + unit + 1] for c in range(CONV)]
                        if j == 0:
                            wait_drained(dve, ("cw",))
                        link(dve.tensor_scalar(sil[:, j, :], ps[:], w[CONV - 1], None, ALU.mult))
                        for back in range(1, CONV):
                            part = sil[:, j, back:S]
                            ins = dve.scalar_tensor_tensor(out=part, in0=ps[:, 0:S - back], scalar=w[CONV - 1 - back],
                                                           in1=part, op0=ALU.mult, op1=ALU.add)
                            if back < CONV - 1:
                                link(ins)
                        ins.then_inc(drain(("T", slot(*UNITS[j]))), 1)
                    elif kind == "bdT":
                        ps = wait_filled(dve, step)
                        dve.tensor_copy(bdT, ps[0:2 * NH, :]).then_inc(drain(step), 1)
                    elif kind == "g1":
                        ps = wait_filled(dve, ("bd",))
                        raw = ps[:, 0:NT * 2 * NH].rearrange("p (t n) -> p t n", t=NT)
                        dve.tensor_tensor(gt["z"][:], raw[:, :, NH:2 * NH], dtb[:].unsqueeze(1).broadcast_to(wide),
                                          ALU.add).then_inc(gate_math, 1)
                        dve.wait_ge(gate_math, 1)
                        link(dve.tensor_scalar(gt["zn"][:], gt["z"][:], -1.0, None, ALU.mult))
                        dve.tensor_tensor(gt["e"][:], gt["z"][:], gt["zn"][:], ALU.min).then_inc(gate_math, 1)
                        dve.tensor_scalar(gt["mz"][:], gt["z"][:], 0.0, None, ALU.max).then_inc(dve_own, 1)
                        own[0] += 1
                    elif kind == "g3":
                        dve.wait_ge(gate_math, 3)
                        dve.wait_ge(dve_own, own[0])
                        link(dve.tensor_tensor(gt["zn"][:], gt["mz"][:], gt["ln"][:], ALU.add))
                        dve.scalar_tensor_tensor(out=gt["g"][:], in0=gt["zn"][:], scalar=-1.0,
                                                 in1=expa[:].unsqueeze(1).broadcast_to(wide), op0=ALU.mult, op1=ALU.mult)\
                           .then_inc(gate_math, 1)
                        wait_drained(dve, ("bd",))
                        link(dve.tensor_scalar(gt["eb"][:], gt["eb"][:], 1.0, None, ALU.add))
                        link(dve.reciprocal(gt["beta"][:], gt["eb"][:]))
                    elif kind == "gc":
                        ps = wait_filled(dve, step)
                        dve.tensor_copy(gcum[:].rearrange("p a t n -> p (a t n)"), ps[:, 0:2 * NT * NH])\
                           .then_inc(drain(step), 1)
                        wait_drained(dve, step)
                        dve.tensor_tensor(gt["gd"][:], gcum[:, 1, :, :], gcum[:, 0, :, :], ALU.subtract)\
                           .then_inc(gate_math, 1)
                    elif kind == "g4":
                        dve.wait_ge(gate_math, 6)
                        dve.tensor_tensor(gt["beg"][:], gt["beta"][:], gt["eg"][:], ALU.mult).then_inc(gate_math, 1)
                    elif kind == "gates":
                        for t in range(NT):
                            wait_drained(dve, ("N", "gate", t))
                            dve.tensor_tensor(per_head(gs[:, t, :]), per_head(gs[:, t, :]),
                                              dnn[:].unsqueeze(1).broadcast_to([P, NH, DH]), ALU.mult)\
                               .then_inc(gate_gained, 1)
                    elif kind == "t1" and step[1] != "v":
                        c, i = step[1:]
                        dve.wait_ge(norm_squared[c], i + 1)
                        ss = ss_qk[:, "kq".index(c), i, :]
                        link(dve.tensor_reduce(ss, (kn if c == "k" else y)[:], AX_X, ALU.add))
                        ins = dve.tensor_scalar(ss, ss, EPS, None, ALU.add)
                        if c == "k":
                            ins.then_inc(k_summed, 1)
                        else:
                            ins.then_inc(drain(step), 1)
                    elif kind == "ks":
                        i = step[1]
                        key = ("t1", "k", i)
                        dve.wait_ge(k_rooted, i + 1)
                        dve.tensor_tensor(kn[:], per_head(bank[USE[key][0]][:]), over(rn_qk[:, 0, i, :]), ALU.mult)\
                           .then_inc(drain(key), 1)
                    elif kind == "t1":
                        i = step[2]
                        ps = wait_filled(dve, step)
                        dve.tensor_tensor(vb[:], per_head(ps[:]), over(gt["beta"][:, i, :]), ALU.mult)\
                           .then_inc(drain(step), 1)
                    elif kind == "gb":
                        i = step[1]
                        dve.wait_ge(bcast_exp, i + 1)
                        ps = bank[USE[step][0]]
                        for h in range(NH):
                            part, own_sum = ps[:, h * P:(h + 1) * P], gcum[:, 0, i, h:h + 1]
                            dve.scalar_tensor_tensor(out=dec[:, h, :], in0=part, scalar=own_sum, in1=neg,
                                                     op0=ALU.subtract, op1=ALU.subtract)
                            ins = dve.scalar_tensor_tensor(out=attnT[:, i % 3, h, :], in0=part, scalar=own_sum,
                                                           in1=negT, op0=ALU.subtract, op1=ALU.add)
                        ins.then_inc(drain(step), 1)
                    elif kind == "kk":
                        i = step[1]
                        ps = wait_filled(dve, step)
                        dve.wait_ge(dec_done, i + 1)
                        if i >= 1:
                            dve.wait_ge(L_done, (LEVELS - 1) * i)
                        for h in range(NH):
                            ins = dve.scalar_tensor_tensor(out=Am[:, h, :], in0=ps[:, h * P:(h + 1) * P],
                                                           scalar=gt["beta"][:, i, h:h + 1], in1=dec[:, h, :],
                                                           op0=ALU.mult, op1=ALU.mult)
                        ins.then_inc(drain(step), 1)
                        wait_drained(dve, step)
                        dve.tensor_tensor(Lm[:, 0, :, :], Am[:], table[:, 5:6, :].broadcast_to([P, NH, P]), ALU.mult)\
                           .then_inc(L0_done, 1)
                    elif kind == "kq":
                        i = step[1]
                        ps = wait_filled(dve, step)
                        dve.wait_ge(dec_done, i + 1)
                        part = attnT[:, i % 3, :, :]
                        dve.tensor_tensor(part, per_head(ps[:]), part, ALU.mult)\
                           .then_inc(drain(step), 1)
                    elif kind == "l1t":
                        i = step[1]
                        ps = wait_filled(dve, step)
                        dve.wait_ge(L0_done, i + 1)
                        dve.tensor_tensor(DiT[:], ident.unsqueeze(1).broadcast_to([P, NH, P]), per_head(ps[:]),
                                          ALU.subtract).then_inc(drain(step), 1)
                        dve.tensor_tensor(Di[:], ident.unsqueeze(1).broadcast_to([P, NH, P]), Lm[:, 0, :, :],
                                          ALU.subtract).then_inc(Di_done, 1)
                    elif kind == "Q":
                        i, lev = step[1:]
                        ps = wait_filled(dve, step)
                        wait_drained(dve, ("Q", i, lev - 1) if lev > 1 else ("l1t", i))
                        for c in range(2):
                            ins = dve.tensor_tensor(blocks(DiT, c), blocks(DiT, c), blocks(per_head(ps[:]), c),
                                                    ALU.subtract)
                        ins.then_inc(drain(step), 1)
                    elif kind == "chA":
                        n = step[1]
                        r = slice(CH * (n % 2), CH * (n % 2) + CH)
                        wait_drained(dve, ("u", n // 2))
                        ps = wait_filled(dve, step)
                        dve.tensor_tensor(vnew[r, :, :], u[r, :, :], ps[r, :].rearrange("p (h c) -> p h c", h=NH),
                                          ALU.subtract).then_inc(drain(step), 1)
                    elif kind == "chS":
                        n = step[1]
                        ps = wait_filled(dve, step)
                        if n == 0:
                            dve.wait_ge(state_zero, 1)
                        else:
                            wait_drained(dve, ("chS", n - 1))
                        for h in range(NH):
                            ins = dve.scalar_tensor_tensor(
                                out=St[:, (n + 1) % 2, h, :], in0=St[:, n % 2, h, :],
                                scalar=egl[:, n // 2 % 3, h, n % 2:n % 2 + 1], in1=ps[:, h * P:(h + 1) * P],
                                op0=ALU.mult, op1=ALU.add)
                        ins.then_inc(drain(step), 1)
                    elif kind == "o1":
                        i = step[1]
                        dve.wait_ge(o_squared, i + 1)
                        dve.wait_ge(q_rooted, i + 1)
                        dve.tensor_tensor(r2_q[:, i, :], rn_qk[:, 1, i, :], rn_qk[:, 1, i, :], ALU.mult)
                        link(dve.tensor_reduce(ss_o[:, i, :], y[:], AX_X, ALU.add))
                        link(dve.scalar_tensor_tensor(out=ms_o[:, i, :], in0=ss_o[:, i, :], scalar=1.0 / DH ** 2,
                                                      in1=r2_q[:, i, :], op0=ALU.mult, op1=ALU.mult))
                        dve.tensor_scalar(ms_o[:, i, :], ms_o[:, i, :], EPS, None, ALU.add).then_inc(o_summed, 1)
                    elif kind == "o2":
                        i = step[1]
                        dve.wait_ge(o_rooted, i + 1)
                        link(dve.scalar_tensor_tensor(out=rs_o[:, i, :], in0=rs_o[:, i, :], scalar=DH ** -0.5,
                                                      in1=rn_qk[:, 1, i, :], op0=ALU.mult, op1=ALU.mult))
                        ps = bank[USE[("PO", i)][0]]
                        dve.tensor_tensor(y[:], per_head(ps[:]), over(rs_o[:, i, :]), ALU.mult)\
                           .then_inc(drain(("PO", i)), 1)
                        wait_drained(dve, ("PO", i))
                        dve.wait_ge(gate_gained, NT)
                        dve.tensor_tensor(y[:], y[:], per_head(gs[:, i, :]), ALU.mult).then_inc(y_done, 1)
                    elif kind == "aS":
                        h, q = step[1:]
                        m, n = NT * h + q, (q + 1) * P
                        ps = wait_filled(dve, step)
                        if q == 0:
                            dve.wait_ge(bias_landed[h % 2], 16 * (h // 2 + 1))
                        dve.tensor_tensor_reduce(out=pr[:, m % 2, 0:n], in0=ps[:, 0:n], in1=ab[:, h % 2, S - n:S],
                                                 scale=-(ADH ** -0.5), scalar=3e38, op0=ALU.add, op1=ALU.min,
                                                 accum_out=nmax[:, m:m + 1]).then_inc(drain(step), 1)
                    elif kind == "aN":
                        h, q = step[1:]
                        m, n = NT * h + q, (q + 1) * P
                        dve.wait_ge(exp_done, m + 1)
                        link(dve.reciprocal(rden[:, m:m + 1], den[:, m:m + 1]))
                        dve.tensor_scalar(pr[:, m % 2, 0:n], pr[:, m % 2, 0:n], rden[:, m:m + 1], None, ALU.mult)\
                           .then_inc(probs_done, 1)
                    elif kind == "aO":
                        ps = wait_filled(dve, ("O", step[1]))
                        dve.tensor_copy(yT[:, step[1], :], ps[:]).then_inc(drain(("O", step[1])), 1)
                    elif kind == "ysplit":
                        k = step[1]
                        dve.wait_ge(y_rounded, (k - AW // P) % KD + 1)
                        dve.tensor_tensor(xT_lo[:, k, :], yT[:, k, :], xT_hi[:, k, :].bitcast(F32), ALU.subtract)\
                           .then_inc(y_split, 1)
                dve.wait_ge(x_back, 16)
            dve.memset(ms_o[:], 0.0).then_inc(split_done, RAWS)
            norm(0)
            ffn(0)
            norm(1, lambda t: add_ffn(0, t))
            mixer()
            norm(2, add_mixer)
            ffn(1)
            for t in range(NT):
                add_ffn(1, t)
                if t >= 1:
                    scale_x(3, t - 1)
            dve.wait_ge(rstd_done, 4 * NT)
            for half in range(2):
                part = slice(half * 512, half * 512 + 512)
                dve.scalar_tensor_tensor(out=xs[:, NT - 1, part], in0=x[:, NT - 1, part],
                                         scalar=rstd[:, 4 * NT - 1:4 * NT], in1=gain[:, part],
                                         op0=ALU.mult, op1=ALU.mult).then_inc(xs_done, 1)

        @block.gpsimd
        def _(pool):
            own = [0]

            def link(ins):
                own[0] += 1
                ins.then_inc(pool_own, 1)
                pool.wait_ge(pool_own, own[0])

            def root(out_ap, in_ap, n):
                return pool.tensor_tensor(out_ap, in_ap, minus_half[:, 0:1].broadcast_to([P, n]), ALU.pow)

            def norm(n):
                for t in range(NT):
                    c = slice(4 * n + t, 4 * n + t + 1)
                    pool.wait_ge(sq_done, NT * n + t + 1)
                    if (n, t) == (3, NT - 1):
                        pool.wait_ge(sq_done, 4 * NT + 1)
                        link(pool.tensor_tensor(ssq[:, c], ssq[:, c], ssq[:, 4 * NT:4 * NT + 1], ALU.add))
                    link(pool.tensor_scalar(ssq[:, c], ssq[:, c], 1.0 / D, EPS, ALU.mult, ALU.add))
                    root(rstd[:, c], ssq[:, c], 1).then_inc(rstd_done, 1)

            def rest_of_slot(w):
                ring = w % SPLITS
                pool.wait_ge(hi_done, w + 1)
                pool.tensor_tensor(w_lo[:, ring, :], w_raw[:, ring % RAWS, :], w_hi[:, ring, :].bitcast(F32),
                                   ALU.subtract).then_inc(split_done, 1)

            def first_rest_of_h(f):
                pool.wait_ge(h_rounded, f * KF + 1)
                pool.tensor_tensor(h_lo[:, 0, :], hT[:, 0, :], h_hi[:, 0, :].bitcast(F32), ALU.subtract)\
                    .then_inc(h_split, 1)

            def mask(i, lev):
                if lev == 1:
                    wait_drained(pool, ("kk", i))
                if lev == 2:
                    pool.wait_ge(Di_done, i + 1)
                    wait_filled(pool, ("l1t", i))
                if lev >= 3:
                    wait_filled(pool, ("W", i, lev - 2))
                pool.tensor_tensor(Lm[:, lev % 2, :, :], Am[:],
                                   table[:, 5 + lev:6 + lev, :].broadcast_to([P, NH, P]), ALU.mult).then_inc(L_done, 1)

            def mixer():
                pool.wait_ge(tables_landed, 16)
                pool.wait_ge(split_done, MBASE + AHEAD + RAWS)
                wait_filled(pool, ("cw",))
                pool.wait_ge(xs_done, 2 * NT)
                wait_filled(pool, ("xT", 1, NT - 1, 1))
                pool.memset(St[:, 0, :, :], 0.0).then_inc(state_zero, 1)
                for step in ORDER:
                    kind = step[0]
                    if kind == "fill" and step[2] == 0:
                        rest_of_slot(MBASE + step[1] + AHEAD)
                    elif kind == "last" and step[1] < AHEAD:
                        rest_of_slot(BASE[1] + step[1])
                    elif kind == "t1" and step[1] == "k":
                        i = step[2]
                        pool.wait_ge(k_summed, i + 1)
                        root(rn_qk[:, 0, i, :], ss_qk[:, 0, i, :], NH).then_inc(k_rooted, 1)
                    elif kind == "t1" and step[1] == "q":
                        i = step[2]
                        wait_drained(pool, step)
                        root(rn_qk[:, 1, i, :], ss_qk[:, 1, i, :], NH).then_inc(q_rooted, 1)
                    elif kind == "ks":
                        i = step[1]
                        wait_drained(pool, ("t1", "k", i))
                        if i == 0:
                            pool.wait_ge(gate_math, 7)
                        if i >= 2:
                            wait_filled(pool, ("w", i - 2))
                            wait_filled(pool, ("chS", 2 * i - 3))
                        pool.tensor_tensor(kbeg[:, i % 2, :, :], kn[:], over(gt["beg"][:, i, :]), ALU.mult)\
                            .then_inc(k_scaled, 1)
                        pool.tensor_tensor(kdec[:, i % 2, :, :], kn[:], over(gt["ekd"][:, i, :]), ALU.mult)\
                            .then_inc(k_scaled, 1)
                    elif kind == "qg":
                        i = step[1]
                        first = unit("dq")
                        wait_silu(pool, "dq")
                        pool.wait_ge(bcast_exp, i + 1)
                        part = qgT[:, i % 3, :, :]
                        pool.tensor_tensor(part, sil[:, first:first + NH, i * P:(i + 1) * P], part, ALU.mult)\
                            .then_inc(q_decayed, 1)
                    elif kind == "kk":
                        mask(step[1], 1)
                    elif kind == "W" and step[2] < LEVELS - 1:
                        mask(step[1], step[2] + 1)
                    elif kind == "o1":
                        i = step[1]
                        pool.wait_ge(o_summed, i + 1)
                        root(rs_o[:, i, :], ms_o[:, i, :], NH).then_inc(o_rooted, 1)

            pool.memset(minus_half[:], -0.5).then_inc(half_set, 1)
            pool.wait_ge(half_set, 1)
            norm(0)
            first_rest_of_h(0)
            norm(1)
            mixer()
            norm(2)
            first_rest_of_h(1)
            norm(3)

        @block.tensor
        def _(pe):
            def three(ps, s_hi, s_lo, m_hi, m_lo, start, stop):
                first = pe.matmul(ps, s_hi, m_hi, start=start, stop=False)
                pe.matmul(ps, s_hi, m_lo, start=False, stop=False)
                return first, pe.matmul(ps, s_lo, m_hi, start=False, stop=stop)

            def transpose_x(n, t):
                pe.wait_ge(xs_done, NT * n + t + 1)
                for half in range(2):
                    key = ("xT", n, t, half)
                    ps = open_bank(pe, key)
                    for j in range(4):
                        k = 4 * half + j
                        ins = pe.transpose(ps[:, j * P:(j + 1) * P], xs[:, t, k * P:(k + 1) * P], ident)
                    ins.then_inc(full(key), 1)

            def x_split(n, tiles):
                for t in tiles:
                    for half in range(2):
                        wait_drained(pe, ("xT", n, t, half))

            def product_T(ps, r, tokens=slice(0, S), begin=True):
                for k in range(KD):
                    s = slice(k * P, (k + 1) * P)
                    first, last = three(ps[:, tokens], w_hi[:, r, s], w_lo[:, r, s], xT_hi[:, k, tokens],
                                        xT_lo[:, k, tokens], k == 0, k == KD - 1)
                    if k == 0 and begin:
                        first.then_inc(slots_begun, 1)
                return last

            def start_with_halves(n, w, banks, fills):
                x_split(n, (0, 1))
                for g in range(2):
                    pe.wait_ge(split_done, w + g + 1 + RAWS)
                    product_T(banks[g], (w + g) % SPLITS, slice(0, S // 2), begin=g == 0)
                    if g == 0:
                        transpose_x(n, 2)
                        transpose_x(n, 3)
                x_split(n, (2, 3))
                for g in range(2):
                    last = product_T(banks[g], (w + g) % SPLITS, slice(S // 2, S), begin=g == 1)
                    last.then_inc(fills[g], 1)

            def ffn(f):
                b, n = BASE[f], UP_BASE[f]
                start_with_halves(2 * f, b, bank[0:2], filled[0:2])
                for g in range(2):
                    k0 = 2 + g
                    pe.wait_ge(split_done, b + 2 + g + 1 + RAWS)
                    last = product_T(bank[k0], (b + 2 + g) % SPLITS)
                    last.then_inc(filled[k0], 1)
                with pe.Fori(1, KF // 2) as i:
                    for c in range(2):
                        for g in range(2):
                            w, k0 = b + 2 * c + g, 2 * c + g
                            pe.wait_ge(split_done, 4 * i + (w + 1 + RAWS))
                            pe.wait_ge(drained[k0], i + n[k0])
                            product_T(bank[k0], w % SPLITS).then_inc(filled[k0], 1)
                b, h0 = BASE[f] + 2 * KF, f * KF

                def step(kt, t, start=False, stop=False, begins=False, halves=(0, 1)):
                    r = (b + kt) % SPLITS
                    hh, hl = (v[:, kt % 2, t * P:(t + 1) * P] for v in (h_hi, h_lo))
                    for part, (s, m) in enumerate(((hh, w_hi), (hh, w_lo), (hl, w_hi))):
                        for half in halves:
                            ins = pe.matmul(bank[2 * t + half][:], s, m[:, r, half * 512:(half + 1) * 512],
                                            start=start and part == 0, stop=stop and part == 2)
                            if begins and part == 0 and half == 0:
                                ins.then_inc(slots_begun, 1)
                            if stop and part == 2:
                                ins.then_inc(filled[2 * t + half], 1)

                def whole(kt, value_slot, value_h, start=False):
                    pe.wait_ge(split_done, value_slot)
                    pe.wait_ge(h_split, value_h)
                    for t in (2, 3, 0, 1):
                        if start:
                            for half in range(2):
                                open_bank(pe, ("y", f, t, half))
                        step(kt, t, start=start, begins=t == 2)

                for kt in range(2):
                    whole(kt, b + kt + 1 + RAWS, h0 + kt + 1, start=kt == 0)
                with pe.Fori(0, 4) as i:
                    for c in range(4):
                        whole(2 + c, 4 * i + (b + 2 + c + 1 + RAWS), 4 * i + (h0 + 2 + c + 1))
                for kt in (18, 19):
                    whole(kt, b + kt + 1 + RAWS, h0 + kt + 1)
                pe.wait_ge(split_done, b + KF - 1 + RAWS)
                pe.wait_ge(h_split, h0 + KF - 1)
                for t in range(NT - f):
                    step(KF - 2, t, begins=t == 0)
                    if t == 0:
                        pe.wait_ge(split_done, b + KF + RAWS)
                        pe.wait_ge(h_split, h0 + KF)
                    if f == 0 and t == 3:
                        transpose_x(1, 1)
                    step(KF - 1, t, stop=True, begins=t == NT - 1)
                    if f == 0 and t == 2:
                        transpose_x(1, 0)
                if f == 1:
                    for half in range(2):
                        step(KF - 2, NT - 1, halves=(half,))
                        step(KF - 1, NT - 1, stop=True, halves=(half,))

            def tiles(j, quarter):
                late = MSLOTS[j][2] in (0, 2) and MSLOTS[j - 1][0] == "T"
                return (0, 1) if (quarter % 2 == 0) != late else (2, 3)

            def fill(j, quarter):
                w = MBASE + j
                r = w % SPLITS
                what, sec, n = MSLOTS[j]
                if quarter == 0:
                    pe.wait_ge(split_done, w + 1 + RAWS)
                if what == "T" and j < 2:
                    return
                if what == "T":
                    key = ("T", j)
                    ps = open_bank(pe, key) if quarter == 0 else bank[USE[key][0]]
                    for k in (2 * quarter, 2 * quarter + 1):
                        s = slice(k * P, (k + 1) * P)
                        first, last = three(ps[:], w_hi[:, r, s], w_lo[:, r, s], xT_hi[:, k, :], xT_lo[:, k, :],
                                            k == 0, k == KD - 1)
                        if k == 0:
                            first.then_inc(slots_begun, 1)
                    if quarter == 3:
                        last.then_inc(full(key), 1)
                    return
                kk = quarter // 2
                k = 2 * n + kk
                k_first, k_last = (0, KD - 1) if what == "N" else (4, 3)
                if what == "O" and quarter == 0:
                    pe.wait_ge(y_split, {2: 2, 3: 4, 0: 6, 1: 8}[n])
                for t in tiles(j, quarter):
                    key = ("N", sec, t) if what == "N" else ("o", sec, t)
                    ps = open_bank(pe, key) if k == k_first else bank[USE[key][0]]
                    s = slice(t * P, (t + 1) * P)
                    m = slice(kk * 512, (kk + 1) * 512)
                    first, last = three(ps[:], xT_hi[:, k, s], xT_lo[:, k, s], w_hi[:, r, m], w_lo[:, r, m],
                                        k == k_first, k == k_last)
                    if quarter == 0 and t == tiles(j, 0)[0]:
                        first.then_inc(slots_begun, 1)
                    if k == k_last:
                        last.then_inc(full(key), 1)

            def last_slots(t):
                for j in (len(MSLOTS) - 2, len(MSLOTS) - 1):
                    _, sec, n = MSLOTS[j]
                    w = MBASE + j
                    if t == 0:
                        pe.wait_ge(split_done, w + 1 + RAWS)
                        pe.wait_ge(y_split, 8)
                    for kk in range(2):
                        k = 2 * n + kk
                        s, m = slice(t * P, (t + 1) * P), slice(kk * 512, (kk + 1) * 512)
                        key = ("o", sec, t)
                        first, last = three(bank[USE[key][0]][:], xT_hi[:, k, s], xT_lo[:, k, s],
                                            w_hi[:, w % SPLITS, m], w_lo[:, w % SPLITS, m], False, k == 3)
                        if kk == 0 and (t, j) in ((0, len(MSLOTS) - 2), (NT - 1, len(MSLOTS) - 1)):
                            first.then_inc(slots_begun, 1)
                        if k == 3:
                            last.then_inc(full(key), 1)
                    if j == len(MSLOTS) - 2 and t == 3:
                        transpose_x(2, 1)
                if t == 2:
                    transpose_x(2, 0)

            def heads(step, product):
                ps = open_bank(pe, step)
                for h in range(NH):
                    ins = product(ps[:, h * P:(h + 1) * P], h)
                ins.then_inc(full(step), 1)

            def in_chunks(step, s, m):
                ps = open_bank(pe, step)
                for h in range(NH):
                    for c in range(2):
                        r = slice(c * CH, (c + 1) * CH)
                        ins = one(ps[r, h * P + c * CH:h * P + (c + 1) * CH], s[r, h, r], m[r, h, r])
                ins.then_inc(full(step), 1)

            def one(ps, s, m):
                return pe.matmul(ps, s, m, start=True, stop=True)

            def mixer():
                pe.wait_ge(tables_landed, 16)
                start_with_halves(1, MBASE, bank[0:2], filled[0:2])
                ps = open_bank(pe, ("cw",))
                n = CONV * len(UNITS)
                pe.wait_ge(small_landed, 16 * 5)
                pe.transpose(ps[:, 0:n], conv_rows[:], table[0:n, 0, 0:n]).then_inc(full(("cw",)), 1)

                for step in ORDER:
                    kind = step[0]
                    if kind == "fill":
                        fill(step[1], step[2])
                    elif kind == "last":
                        last_slots(step[1])
                    elif kind == "bdT":
                        pe.wait_ge(small_split, 2)
                        ps = open_bank(pe, step)
                        for k in range(KD):
                            _, last = three(ps[0:2 * NH, :], wbd_hi[:, k, :], wbd_lo[:, k, :], xT_hi[:, k, :],
                                            xT_lo[:, k, :], k == 0, k == KD - 1)
                        last.then_inc(full(step), 1)
                    elif kind == "bd":
                        wait_drained(pe, ("bdT",))
                        ps = open_bank(pe, step)
                        n = 2 * NH
                        for t in range(NT):
                            ins = pe.transpose(ps[:, t * n:(t + 1) * n], bdT[:, t * P:(t + 1) * P], table[0:n, 0, 0:n])
                        ins.then_inc(full(step), 1)
                    elif kind == "gc":
                        ps = open_bank(pe, step)
                        pe.wait_ge(gate_math, 4)
                        g = gt["g"][:].rearrange("p t n -> p (t n)")
                        one(ps[:, 0:NT * NH], upto, g)
                        one(ps[:, NT * NH:2 * NT * NH], same, g).then_inc(full(step), 1)
                    elif kind == "t1":
                        c, i = step[1:]
                        first = unit("d" + c)
                        wait_silu(pe, "d" + c)
                        heads(step, lambda ps, h: pe.transpose(ps, sil[:, first + h, i * P:(i + 1) * P], ident))
                    elif kind == "t2":
                        i = step[1]
                        wait_drained(pe, ("t1", "k", i))
                        heads(step, lambda ps, h: pe.transpose(ps, kn[:, h, :], ident))
                    elif kind == "gb":
                        i = step[1]
                        heads(step, lambda ps, h: one(ps, gt["g"][:, i, h:h + 1].broadcast_to([P, P]), upto))
                    elif kind in ("kk", "kq"):
                        i = step[1]
                        wait_drained(pe, ("t2", i))
                        cols = slice(i * P, (i + 1) * P)
                        k0, other = unit("dk"), unit("d" + kind[1])
                        if kind == "kq":
                            wait_silu(pe, "dq")
                        heads(step, lambda ps, h: one(ps, sil[:, k0 + h, cols], sil[:, other + h, cols]))
                    elif kind == "l1t":
                        i = step[1]
                        pe.wait_ge(L0_done, i + 1)
                        heads(step, lambda ps, h: pe.transpose(ps, Lm[:, 0, h, :], ident))
                    elif kind == "W":
                        i, lev = step[1:]
                        pe.wait_ge(L_done, (LEVELS - 1) * i + lev)
                        wait_drained(pe, ("Q", i, lev - 1) if lev > 1 else ("l1t", i))
                        in_chunks(step, Lm[:, lev % 2, :, :], DiT)
                    elif kind == "Q":
                        i, lev = step[1:]
                        wait_drained(pe, ("W", i, lev))
                        if lev > 1:
                            wait_drained(pe, ("D", i, lev - 1))
                        else:
                            pe.wait_ge(Di_done, i + 1)
                        in_chunks(step, Di, Wm)
                    elif kind == "D":
                        wait_drained(pe, ("Q", *step[1:]))
                        heads(step, lambda ps, h: pe.transpose(ps, DiT[:, h, :], ident))
                    elif kind == "uw":
                        i = step[1]
                        wait_drained(pe, ("Q", i, LEVELS - 1))
                        wait_drained(pe, ("t1", "v", i))
                        heads(("u", i), lambda ps, h: one(ps, DiT[:, h, :], vb[:, h, :]))
                        pe.wait_ge(k_scaled, 2 * i + 1)
                        heads(("w", i), lambda ps, h: one(ps, kbeg[:, i % 2, h, :], DiT[:, h, :]))
                    elif kind == "chA":
                        n = step[1]
                        r = slice(CH * (n % 2), CH * (n % 2) + CH)
                        wait_drained(pe, ("w", n // 2))
                        if n == 0:
                            pe.wait_ge(state_zero, 1)
                        else:
                            wait_drained(pe, ("chS", n - 1))
                        ps = open_bank(pe, step)
                        for h in range(NH):
                            ins = one(ps[r, h * DH:(h + 1) * DH], wT[:, h, r], St[:, n % 2, h, :])
                        ins.then_inc(full(step), 1)
                    elif kind == "chS":
                        n = step[1]
                        r = slice(CH * (n % 2), CH * (n % 2) + CH)
                        wait_drained(pe, ("chA", n))
                        pe.wait_ge(k_scaled, 2 * (n // 2) + 2)
                        heads(step, lambda ps, h: one(ps, kdec[r, n // 2 % 2, h, :], vnew[r, h, :]))
                    elif kind == "chO":
                        n = step[1]
                        i = n // 2
                        r = slice(CH * (n % 2), CH * (n % 2) + CH)
                        pe.wait_ge(q_decayed, i + 1)
                        wait_drained(pe, ("kq", i))
                        key = ("PO", i)
                        ps = open_bank(pe, key) if n % 2 == 0 else bank[USE[key][0]]
                        for h in range(NH):
                            cols = slice(h * DH, (h + 1) * DH)
                            pe.matmul(ps[r, cols], qgT[:, i % 3, h, r], St[:, n % 2, h, :], start=True, stop=False)
                            ins = pe.matmul(ps[r, cols], attnT[r, i % 3, h, r], vnew[r, h, :], start=False, stop=True)
                        if n % 2 == 1:
                            ins.then_inc(full(key), 1)
                    elif kind == "outT":
                        pe.wait_ge(y_done, step[1] + 1)
                        heads(step, lambda ps, h: pe.transpose(ps, y[:, h, :], ident))
                    elif kind == "aS":
                        h, q = step[1:]
                        pair, r = h // 2, slice(ADH * (h % 2), ADH * (h % 2) + ADH)
                        wait_drained(pe, ("T", slot("aq", pair)))
                        wait_drained(pe, ("T", slot("ak", pair)))
                        ps = open_bank(pe, step)
                        one(ps[:, 0:(q + 1) * P], qk[r, pair % 2, 0, q * P:(q + 1) * P],
                            qk[r, pair % 2, 1, 0:(q + 1) * P]).then_inc(full(step), 1)
                    elif kind == "aT":
                        h, q = step[1:]
                        m = NT * h + q
                        pe.wait_ge(probs_done, m + 1)
                        ps = open_bank(pe, step)
                        for kb in range(q + 1):
                            ins = pe.transpose(ps[:, kb * P:(kb + 1) * P], pr[:, m % 2, kb * P:(kb + 1) * P], ident)
                        ins.then_inc(full(step), 1)
                    elif kind == "aV":
                        h, q = step[1:]
                        pair, r = h // 2, slice(ADH * (h % 2), ADH * (h % 2) + ADH)
                        key = ("O", pair)
                        ps = open_bank(pe, key) if h % 2 == 0 and q == 0 else bank[USE[key][0]]
                        wait_drained(pe, ("aT", h, q))
                        wait_drained(pe, ("N", "av", NT - 1))
                        for kb in range(q + 1):
                            ins = pe.matmul(ps[r, q * P:(q + 1) * P], av[:, kb, h * ADH:(h + 1) * ADH],
                                            pT[:, q % 2, kb * P:(kb + 1) * P], start=kb == 0, stop=kb == q)
                        if h % 2 == 1 and q == NT - 1:
                            ins.then_inc(full(key), 1)

            pe.wait_ge(ident_landed, 16)
            transpose_x(0, 0)
            transpose_x(0, 1)
            ffn(0)
            mixer()
            ffn(1)


NAMES = ("x", "norm_ffn1", "ffn1_gate", "ffn1_up", "ffn1_down", "norm_mix", "w_in", "conv_w", "a_log", "dt_bias",
         "dn_norm", "w_out", "norm_ffn2", "ffn2_gate", "ffn2_up", "ffn2_down", "norm_final")


def kernel(**inputs):
    import concourse.bacc as bacc
    from concourse.bass_utils import run_bass_kernel_spmd

    nc = bacc.Bacc("TRN2", target_bir_lowering=False, num_devices=1)
    arrays = {name: np.ascontiguousarray(inputs[name]) for name in NAMES}
    arrays["table"], arrays["bias"] = shape_tables()
    handles = {n: nc.dram_tensor("in_" + n, a.shape, mybir.dt.from_np(a.dtype), kind="ExternalInput").ap()
               for n, a in arrays.items()}
    result = nc.dram_tensor("out_0", (1, S, D), F32, kind="ExternalOutput").ap()
    decoder_layer(nc, handles, result)
    r = run_bass_kernel_spmd(nc, [{"in_" + n: a for n, a in arrays.items()}], core_ids=[0])
    return r.results[0]["out_0"]
```
